# Optimizing a Trainium2 kernel written in Bass

```python
import math
import jax, jax.numpy as jnp
from jax import lax
import numpy as np

D_MODEL = 2048
BATCH = 1
SEQ = 128
DEPTH = 2
DEC_BATCH = 1
DEC_SEQ = 128
PAST_LEN = 128

GRID_W = 64
HEAD_DIM = 128
N_Q_HEADS = D_MODEL // HEAD_DIM
N_KV_HEADS = 4
Q_PER_KV = N_Q_HEADS // N_KV_HEADS
ATTN_WIDTH = N_Q_HEADS * HEAD_DIM
KV_WIDTH = N_KV_HEADS * HEAD_DIM
WINDOW = 128
BLOCK = 128
ROPE_BASE = 10000.0
SSD_WIDTH = 2 * D_MODEL
SSD_HEADDIM = 64
N_SSD_HEADS = SSD_WIDTH // SSD_HEADDIM
D_STATE = 128
N_SSD_GROUPS = 8
HEADS_PER_GROUP = N_SSD_HEADS // N_SSD_GROUPS
SSD_CHUNK = 128
D_CONV = 5
BC_WIDTH = N_SSD_GROUPS * D_STATE
CONV_WIDTH = SSD_WIDTH + 2 * BC_WIDTH
EPS = 1e-6
IN_SPLITS = (ATTN_WIDTH, KV_WIDTH, KV_WIDTH, ATTN_WIDTH, CONV_WIDTH, SSD_WIDTH, N_SSD_HEADS, N_SSD_HEADS, D_MODEL, D_MODEL)
IN_WIDTH = 19584

kernel_name = 'bidir_ssd_swa_hybrid_dit_step'

def split_cols(x, sizes):
    offsets = np.cumsum(np.array(sizes))[:-1].tolist()
    return jnp.split(x, offsets, axis=-1)

def rmsnorm(x, g):
    xf = x.astype(jnp.float32)
    y = xf * lax.rsqrt(jnp.mean(xf * xf, axis=-1, keepdims=True) + EPS)
    return (y * g.astype(jnp.float32)).astype(x.dtype)

def axial_rope(x):
    length = x.shape[1]
    rows = length // GRID_W
    t_row = jnp.repeat(jnp.arange(rows), GRID_W)
    t_col = jnp.tile(jnp.arange(GRID_W), rows)
    sec = HEAD_DIM // 2
    half = sec // 2
    freqs = ROPE_BASE ** (-jnp.arange(half, dtype=jnp.float32) / half)

    def rot(xs, pos):
        ang = pos.astype(jnp.float32)[:, None] * freqs[None, :]
        cos = jnp.cos(ang)[None, :, None, :]
        sin = jnp.sin(ang)[None, :, None, :]
        x1 = xs[..., :half].astype(jnp.float32)
        x2 = xs[..., half:].astype(jnp.float32)
        return jnp.concatenate([x1 * cos - x2 * sin, x2 * cos + x1 * sin], axis=-1)

    out = jnp.concatenate([rot(x[..., :sec], t_row), rot(x[..., sec:], t_col)], axis=-1)
    return out.astype(x.dtype)

def centred_conv(u, w, b):
    out = lax.conv_general_dilated(
        u, w[:, None, :].astype(u.dtype), window_strides=(1,),
        padding=[(D_CONV // 2, D_CONV // 2)],
        dimension_numbers=('NWC', 'WIO', 'NWC'),
        feature_group_count=u.shape[-1])
    return out + b.astype(u.dtype)

def mixer_inputs(x, cond, norm_g, w_mod, b_mod, w_in, conv_w, conv_b):
    shift, scale, gate = jnp.split(jax.nn.silu(cond) @ w_mod + b_mod, 3, axis=-1)
    h = rmsnorm(x, norm_g) * (1 + scale) + shift
    q, k, v, z_a, xbc, z_s, dt_f, dt_b, g_a, g_s = split_cols(h @ w_in, IN_SPLITS)
    xbc = jax.nn.silu(centred_conv(xbc, conv_w, conv_b))
    xs, b_ssm, c_ssm = split_cols(xbc, (SSD_WIDTH, BC_WIDTH, BC_WIDTH))
    bsz, length = x.shape[:2]
    q = q.reshape(bsz, length, N_Q_HEADS, HEAD_DIM)
    k = k.reshape(bsz, length, N_KV_HEADS, HEAD_DIM)
    v = v.reshape(bsz, length, N_KV_HEADS, HEAD_DIM)
    return q, k, v, z_a, xs, b_ssm, c_ssm, z_s, dt_f, dt_b, g_a, g_s, gate

def context_attention(q, k, v, sink):
    bsz, lc = q.shape[:2]
    nq = lc // BLOCK
    scale = HEAD_DIM ** -0.5
    qb = q.reshape(bsz, nq, BLOCK, N_KV_HEADS, Q_PER_KV, HEAD_DIM).transpose(1, 0, 2, 3, 4, 5)
    sink_g = sink.astype(jnp.float32).reshape(1, N_KV_HEADS, Q_PER_KV, 1, 1)

    def one_block(qblk):
        s = jnp.einsum('bqgrd,bkgd->bgrqk', qblk, k).astype(jnp.float32) * scale
        sink_col = jnp.broadcast_to(sink_g, s.shape[:-1] + (1,))
        p = jax.nn.softmax(jnp.concatenate([sink_col, s], axis=-1), axis=-1)[..., 1:]
        return jnp.einsum('bgrqk,bkgd->bqgrd', p.astype(v.dtype), v)

    o = lax.map(one_block, qb)
    return o.transpose(1, 0, 2, 3, 4, 5).reshape(bsz, lc, ATTN_WIDTH)

def latent_attention(q, k, v, kc, vc, sink):
    bsz, length = q.shape[:2]
    nb = length // BLOCK
    lc = kc.shape[1]
    scale = HEAD_DIM ** -0.5
    qb = q.reshape(bsz, nb, BLOCK, N_KV_HEADS, Q_PER_KV, HEAD_DIM)
    pad = ((0, 0), (BLOCK, BLOCK), (0, 0), (0, 0))
    kp = jnp.pad(k, pad).reshape(bsz, nb + 2, BLOCK, N_KV_HEADS, HEAD_DIM)
    vp = jnp.pad(v, pad).reshape(bsz, nb + 2, BLOCK, N_KV_HEADS, HEAD_DIM)
    kb = jnp.concatenate([kp[:, :-2], kp[:, 1:-1], kp[:, 2:]], axis=2)
    vb = jnp.concatenate([vp[:, :-2], vp[:, 1:-1], vp[:, 2:]], axis=2)
    qpos = jnp.arange(nb)[:, None] * BLOCK + jnp.arange(BLOCK)[None, :]
    kpos = jnp.arange(nb)[:, None] * BLOCK - BLOCK + jnp.arange(3 * BLOCK)[None, :]
    mask = ((jnp.abs(qpos[:, :, None] - kpos[:, None, :]) <= WINDOW)
            & (kpos[:, None, :] >= 0) & (kpos[:, None, :] < length))
    s_lat = jnp.einsum('bnqgrd,bnkgd->bngrqk', qb, kb).astype(jnp.float32) * scale
    s_lat = jnp.where(mask[None, :, None, None], s_lat, -jnp.inf)
    s_ctx = jnp.einsum('bnqgrd,bkgd->bngrqk', qb, kc).astype(jnp.float32) * scale
    sink_col = jnp.broadcast_to(sink.astype(jnp.float32).reshape(1, 1, N_KV_HEADS, Q_PER_KV, 1, 1),
                                s_ctx.shape[:-1] + (1,))
    p = jax.nn.softmax(jnp.concatenate([sink_col, s_ctx, s_lat], axis=-1), axis=-1)
    p_ctx = p[..., 1:1 + lc].astype(v.dtype)
    p_lat = p[..., 1 + lc:].astype(v.dtype)
    o = (jnp.einsum('bngrqk,bkgd->bnqgrd', p_ctx, vc)
         + jnp.einsum('bngrqk,bnkgd->bnqgrd', p_lat, vb))
    return o.reshape(bsz, length, ATTN_WIDTH)

def ssd_scan(x, dt, a, bm, cm, s0):
    f32 = jnp.float32
    bsz, length = x.shape[:2]
    nc = length // SSD_CHUNK
    g, r, q = N_SSD_GROUPS, HEADS_PER_GROUP, SSD_CHUNK
    xc = x.astype(f32).reshape(bsz, nc, q, g, r, SSD_HEADDIM)
    dtc = dt.reshape(bsz, nc, q, g, r)
    bc = bm.astype(f32).reshape(bsz, nc, q, g, D_STATE)
    cc = cm.astype(f32).reshape(bsz, nc, q, g, D_STATE)
    acs = jnp.cumsum(dtc * a.reshape(g, r), axis=2)
    acs_t = jnp.moveaxis(acs, 2, -1)
    seg = acs_t[..., :, None] - acs_t[..., None, :]
    lower = jnp.tril(jnp.ones((q, q), dtype=bool))
    decay_in = jnp.exp(jnp.where(lower, seg, -jnp.inf))
    cb = jnp.einsum('bcign,bcjgn->bcgij', cc, bc)
    xdt = xc * dtc[..., None]
    y_diag = jnp.einsum('bcgij,bcgrij,bcjgrp->bcigrp', cb, decay_in, xdt)
    acs_last = acs[:, :, -1]
    decay_to_end = jnp.exp(acs_last[:, :, None] - acs)
    chunk_states = jnp.einsum('bcjgn,bcjgr,bcjgrp->bcgrpn', bc, decay_to_end, xdt)
    chunk_decay = jnp.exp(acs_last)

    def step(s, inp):
        dec, st = inp
        return s * dec[..., None, None] + st, s

    s_init = s0.astype(f32).reshape(bsz, g, r, SSD_HEADDIM, D_STATE)
    s_final, s_starts = lax.scan(step, s_init, (jnp.moveaxis(chunk_decay, 1, 0),
                                                 jnp.moveaxis(chunk_states, 1, 0)))
    s_starts = jnp.moveaxis(s_starts, 0, 1)
    y_off = jnp.einsum('bcign,bcgrpn,bcigr->bcigrp', cc, s_starts, jnp.exp(acs))
    y = (y_diag + y_off).reshape(bsz, length, N_SSD_HEADS, SSD_HEADDIM)
    return y.astype(x.dtype), s_final.reshape(bsz, N_SSD_HEADS, SSD_HEADDIM, D_STATE).astype(x.dtype)

def ssd_branch(xs, b_ssm, c_ssm, z_s, dt_f, dt_b, s0_f, s0_b,
               a_log_f, a_log_b, dt_bias_f, dt_bias_b, d_skip, ssd_norm_g):
    bsz, length = xs.shape[:2]
    f32 = jnp.float32
    x4 = xs.reshape(bsz, length, N_SSD_HEADS, SSD_HEADDIM)
    bm = b_ssm.reshape(bsz, length, N_SSD_GROUPS, D_STATE)
    cm = c_ssm.reshape(bsz, length, N_SSD_GROUPS, D_STATE)
    dtf = jax.nn.softplus(dt_f.astype(f32) + dt_bias_f.astype(f32))
    dtb = jax.nn.softplus(dt_b.astype(f32) + dt_bias_b.astype(f32))
    a_f = -jnp.exp(a_log_f.astype(f32))
    a_b = -jnp.exp(a_log_b.astype(f32))
    y_f, s_f = ssd_scan(x4, dtf, a_f, bm, cm, s0_f)
    y_b, s_b = ssd_scan(jnp.flip(x4, 1), jnp.flip(dtb, 1), a_b, jnp.flip(bm, 1), jnp.flip(cm, 1), s0_b)
    y = y_f + jnp.flip(y_b, 1) + d_skip[:, None].astype(x4.dtype) * x4
    y = y.reshape(bsz, length, SSD_WIDTH) * jax.nn.silu(z_s)
    yg = rmsnorm(y.reshape(bsz, length, N_SSD_GROUPS, SSD_WIDTH // N_SSD_GROUPS),
                 ssd_norm_g.reshape(N_SSD_GROUPS, SSD_WIDTH // N_SSD_GROUPS))
    return yg.reshape(bsz, length, SSD_WIDTH), s_f, s_b

def merge(x, o_a, z_a, y_s, g_a, g_s, gate, w_pa, w_ps, w_out):
    branch_a = (o_a * jax.nn.silu(z_a)) @ w_pa
    branch_s = y_s @ w_ps
    merged = jax.nn.sigmoid(g_a) * branch_a + jax.nn.sigmoid(g_s) * branch_s
    return x + gate * (merged @ w_out)

def setup_inputs(seed: int = 0) -> dict:
    key = jax.random.key(seed)
    ks = jax.random.split(key, 26)
    f32 = jnp.float32

    def nrm(k, shape, scale):
        return jax.random.normal(k, shape, f32) * scale

    def dt_bias_init(k):
        dt = jnp.exp(jax.random.uniform(k, (DEPTH, N_SSD_HEADS), f32, math.log(1e-3), math.log(1e-1)))
        return dt + jnp.log(-jnp.expm1(-dt))

    return {
        'x_prompt': nrm(ks[0], (BATCH, SEQ, D_MODEL), 1.0),
        'x_sample': nrm(ks[1], (DEC_BATCH, DEC_SEQ, D_MODEL), 1.0),
        'c': nrm(ks[2], (DEC_BATCH, D_MODEL), 1.0),
        'cache_k': nrm(ks[3], (DEC_BATCH, DEPTH, PAST_LEN, N_KV_HEADS, HEAD_DIM), 1.0),
        'cache_v': nrm(ks[4], (DEC_BATCH, DEPTH, PAST_LEN, N_KV_HEADS, HEAD_DIM), 1.0),
        'state_ssm_fwd': nrm(ks[5], (DEC_BATCH, DEPTH, N_SSD_HEADS, SSD_HEADDIM, D_STATE), 0.1),
        'state_ssm_bwd': nrm(ks[6], (DEC_BATCH, DEPTH, N_SSD_HEADS, SSD_HEADDIM, D_STATE), 0.1),
        'c_ctx': nrm(ks[7], (D_MODEL,), 1.0),
        'norm_g': 1.0 + nrm(ks[8], (DEPTH, D_MODEL), 0.02),
        'w_mod': nrm(ks[9], (DEPTH, D_MODEL, 3 * D_MODEL), 0.5 * D_MODEL ** -0.5),
        'b_mod': nrm(ks[10], (DEPTH, 3 * D_MODEL), 0.02),
        'w_in': nrm(ks[11], (DEPTH, D_MODEL, IN_WIDTH), D_MODEL ** -0.5),
        'conv_w': nrm(ks[12], (DEPTH, D_CONV, CONV_WIDTH), D_CONV ** -0.5),
        'conv_b': nrm(ks[13], (DEPTH, CONV_WIDTH), 0.02),
        'attn_sink': nrm(ks[14], (DEPTH, N_Q_HEADS), 1.0),
        'a_log_fwd': jnp.log(jax.random.uniform(ks[15], (DEPTH, N_SSD_HEADS), f32, 1.0, 16.0)),
        'a_log_bwd': jnp.log(jax.random.uniform(ks[16], (DEPTH, N_SSD_HEADS), f32, 1.0, 16.0)),
        'dt_bias_fwd': dt_bias_init(ks[17]),
        'dt_bias_bwd': dt_bias_init(ks[18]),
        'd_skip': 1.0 + nrm(ks[19], (DEPTH, N_SSD_HEADS), 0.02),
        'ssd_norm_g': 1.0 + nrm(ks[20], (DEPTH, SSD_WIDTH), 0.02),
        'w_pa': nrm(ks[21], (DEPTH, ATTN_WIDTH, D_MODEL), ATTN_WIDTH ** -0.5),
        'w_ps': nrm(ks[22], (DEPTH, SSD_WIDTH, D_MODEL), SSD_WIDTH ** -0.5),
        'w_out': nrm(ks[23], (DEPTH, D_MODEL, D_MODEL), D_MODEL ** -0.5),
        'final_norm_g': 1.0 + nrm(ks[24], (D_MODEL,), 0.02),
    }

def reference(x_prompt, x_sample, c, cache_k, cache_v, state_ssm_fwd, state_ssm_bwd, c_ctx,
              norm_g, w_mod, b_mod, w_in, conv_w, conv_b, attn_sink, a_log_fwd, a_log_bwd,
              dt_bias_fwd, dt_bias_bwd, d_skip, ssd_norm_g, w_pa, w_ps, w_out, final_norm_g):
    xp = x_prompt
    xl = x_sample
    bsz_p = x_prompt.shape[0]
    new_k, new_v, new_sf, new_sb = [], [], [], []
    for l in range(DEPTH):
        q, k, v, z_a, xs, b_ssm, c_ssm, z_s, dt_f, dt_b, g_a, g_s, gate = mixer_inputs(
            xp, c_ctx[None, None, :], norm_g[l], w_mod[l], b_mod[l], w_in[l], conv_w[l], conv_b[l])
        o_a = context_attention(q, k, v, attn_sink[l])
        zero_state = jnp.zeros((bsz_p, N_SSD_HEADS, SSD_HEADDIM, D_STATE), xp.dtype)
        y_s, s_f, s_b = ssd_branch(xs, b_ssm, c_ssm, z_s, dt_f, dt_b, zero_state, zero_state,
                                   a_log_fwd[l], a_log_bwd[l], dt_bias_fwd[l], dt_bias_bwd[l],
                                   d_skip[l], ssd_norm_g[l])
        xp = merge(xp, o_a, z_a, y_s, g_a, g_s, gate, w_pa[l], w_ps[l], w_out[l])
        new_k.append(k)
        new_v.append(v)
        new_sf.append(s_f)
        new_sb.append(s_b)
        q, k, v, z_a, xs, b_ssm, c_ssm, z_s, dt_f, dt_b, g_a, g_s, gate = mixer_inputs(
            xl, c[:, None, :], norm_g[l], w_mod[l], b_mod[l], w_in[l], conv_w[l], conv_b[l])
        o_a = latent_attention(axial_rope(q), axial_rope(k), v, cache_k[:, l], cache_v[:, l], attn_sink[l])
        y_s, _, _ = ssd_branch(xs, b_ssm, c_ssm, z_s, dt_f, dt_b, state_ssm_fwd[:, l], state_ssm_bwd[:, l],
                               a_log_fwd[l], a_log_bwd[l], dt_bias_fwd[l], dt_bias_bwd[l],
                               d_skip[l], ssd_norm_g[l])
        xl = merge(xl, o_a, z_a, y_s, g_a, g_s, gate, w_pa[l], w_ps[l], w_out[l])
    y_prompt = rmsnorm(xp, final_norm_g)
    y_sample = rmsnorm(xl, final_norm_g)
    new_cache_k = jnp.stack(new_k, axis=1)
    new_cache_v = jnp.stack(new_v, axis=1)
    new_state_ssm_fwd = jnp.stack(new_sf, axis=1)
    new_state_ssm_bwd = jnp.stack(new_sb, axis=1)
    return (y_prompt, y_sample, new_cache_k, new_cache_v, new_state_ssm_fwd, new_state_ssm_bwd)


_drawn_inputs = setup_inputs


def setup_inputs(seed=0):
    import zlib

    import numpy as np

    out = dict(_drawn_inputs(seed))
    spreads = {}
    factors = {'cache_k': 5.659,
     'cache_v': 4.789,
     'attn_sink': 8.0,
     'd_skip': 8.0,
     'ssd_norm_g': 8.0,
     'final_norm_g': 2.823}
    for name, (base, spread) in spreads.items():
        noise = np.random.default_rng([zlib.crc32(name.encode()), seed]).standard_normal(out[name].shape)
        drawn = base * np.exp(spread * noise) if base else spread * noise
        out[name] = __import__('jax').numpy.asarray(drawn.astype(out[name].dtype))
    for name, factor in factors.items():
        out[name] = (out[name] * factor).astype(out[name].dtype)
    return out
```

```python
from contextlib import ExitStack

import concourse.bass as bass
from concourse import mybir

F32 = mybir.dt.float32
F32R = mybir.dt.float32r
BF16 = mybir.dt.bfloat16
ACT = mybir.ActivationFunctionType
ALU = mybir.AluOpType
AX_X = mybir.AxisListType.X

P = 128
D_MODEL = 2048
DEPTH = 2
TOK = 128
HEAD_DIM = 128
N_Q = 16
N_KV = 4
KV_WIDTH = N_KV * HEAD_DIM
SSD_WIDTH = 2 * D_MODEL
HP = 64
NH = SSD_WIDTH // HP
NG = 8
HG = NH // NG
D_STATE = 128
BC_WIDTH = NG * D_STATE
D_CONV = 5
EPS = 1e-6
SCALE = HEAD_DIM ** -0.5
N = 512
KT = D_MODEL // P
IN_SPLITS = (D_MODEL, KV_WIDTH, KV_WIDTH, D_MODEL, SSD_WIDTH + 2 * BC_WIDTH, SSD_WIDTH, 2 * NH, D_MODEL, D_MODEL)
C_Q, C_K, C_V, C_ZA, C_XBC, C_ZS, C_DT, C_GA, C_GS = [sum(IN_SPLITS[:i]) for i in range(9)]
C_BC = C_XBC + SSD_WIDTH
IN_WIDTH = sum(IN_SPLITS)

NMOD = 3 * D_MODEL // N
PH_MOD = 0
PH_DT = PH_MOD + NMOD
PH_BC = PH_DT + 1
PH_SSD = PH_BC + 4
PH_PS = PH_SSD + 2 * NG
PH_KV = PH_PS + 4 * 3
PH_Q = PH_KV + 2
PH_PA = PH_Q + 8
PH_OUT = PH_PA + 8
CHUNKS = PH_OUT + 4
U_MOD = 0
U_BC = U_MOD + NMOD // 2
U_SSD = U_BC + 2
U_PS = U_SSD + NG
U_KV = U_PS + 4
U_Q = U_KV + 1
U_PA = U_Q + 4
U_OUT = U_PA + 4
USES = U_OUT + 2
PHASES = 9
NQ = 17

K_ID, K_U, K_L, K_COS, K_SIN, K_NEG, K_SEL, K_COMB, K_WIDTH = 0, 128, 256, 384, 512, 640, 896, 904, 906


def constants():
    import numpy as np

    k = np.zeros((P, K_WIDTH), np.float32)
    t = np.arange(P)
    k[:, K_ID:K_ID + P] = np.eye(P)
    k[:, K_U:K_U + P] = t[:, None] <= t[None, :]
    k[:, K_L:K_L + P] = t[:, None] >= t[None, :]
    half = HEAD_DIM // 4
    freqs = (np.float32(10000.0) ** (-np.arange(half, dtype=np.float32) / np.float32(half))).astype(np.float32)
    for sec, pos in enumerate((t // 64, t % 64)):
        ang = pos.astype(np.float32)[:, None] * freqs[None, :]
        for hf, sign in enumerate((-1.0, 1.0)):
            at = sec * 64 + hf * 32
            k[:, K_COS + at:K_COS + at + 32] = np.cos(ang)
            k[:, K_SIN + at:K_SIN + at + 32] = sign * np.sin(ang)
    k[:, K_NEG:K_NEG + P] = np.where(t[:, None] > t[None, :], -1e30, 0.0)
    k[:, K_NEG + P:K_NEG + 2 * P] = np.where(t[:, None] < t[None, :], -1e30, 0.0)
    for h in range(HG):
        k[h, K_SEL + h] = 1.0
        k[64 + h, K_SEL + h] = 1.0
    for r in range(4):
        k[r, K_COMB + r % 2] = 1.0
    k[4, K_COMB:K_COMB + 2] = 1.0
    return k


class Chain:

    def __init__(self, eng, sem):
        self.eng, self.sem, self.n = eng, sem, 0

    def link(self, ins):
        ins.then_inc(self.sem, 1)
        self.n += 1
        return self.n

    def wait(self, n=None):
        self.eng.wait_ge(self.sem, self.n if n is None else n)

    def reset(self):
        if self.n:
            self.eng.wait_ge(self.sem, self.n)
            self.eng.sem_clear(self.sem)
            self.n = 0


def build(nc, a, o):
    with ExitStack() as ctx:
        def sb(name, shape, dt=F32):
            return ctx.enter_context(nc.sbuf_tensor(name, shape, dt))

        def sem(name):
            return ctx.enter_context(nc.semaphore(name))

        x_dram = nc.dram_tensor("x_scratch", (2, TOK, D_MODEL), F32).ap()
        mod_dram = nc.dram_tensor("mod_scratch", (2, 3 * D_MODEL), F32).ap()

        hT_h = sb("hT_h", [P, KT, 256], F32R)
        hT_l = sb("hT_l", [P, KT, 256], F32R)
        Z = sb("Z", [P, 2, 32, 256], F32R)
        yT_h, yT_l = Z[:, 0], Z[:, 1]
        aT_h, aT_l = Z[:, 0, 0:16], Z[:, 0, 16:32]
        mT_h, mT_l = Z[:, 1, 0:16], Z[:, 1, 16:32]
        raw = sb("raw", [P, 4, 2, N])
        w_h = sb("w_h", [P, 4, 2, N], F32R)
        w_l = sb("w_l", [P, 4, 2, N], F32R)
        X = sb("X", [P, 4096])
        x2 = X[:].rearrange("p (s n) -> p s n", s=2)
        xc = X[:, 0:1024]
        xt = X[:, 1024:2048].rearrange("p (s n) -> p s n", s=2)
        y = X[:, 2048:3072].rearrange("p (s n) -> p s n", s=2)
        zs = X[:, 3072:4096].rearrange("p (s n) -> p s n", s=2)
        arena = sb("arena", [P, 9728])
        used_to = [0]

        def part(n, at=None):
            at = used_to[0] if at is None else at
            used_to[0] = at + n
            assert used_to[0] <= 9728
            return arena[:, at:at + n]

        BC = part(4096, 0).rearrange("p (t n) -> p t n", n=256)
        BCg = part(512).rearrange("p (t n) -> p t n", n=256)
        Bt = part(128)
        CB = part(256).rearrange("p (s n) -> p s n", s=2)
        E = [part(512).rearrange("p (d s n) -> p d s n", d=2, s=2) for _ in range(2)]
        xw = part(1024).rearrange("p (d n) -> p d n", d=2)
        ST = part(1024).rearrange("p (d n) -> p d n", d=2)
        stload = part(1024).rearrange("p (d t n) -> p d t n", d=2, t=4)
        yoff = stload[:, 0].rearrange("p t n -> p (t n)")
        h32 = [part(1024, 0), part(1024)]
        modrow = [part(512), part(512)]
        modfin = [part(512), part(512)]
        rows = part(384).rearrange("p (t n) -> p t n", t=3)
        sq_dump = part(2048)
        dtz, dte, dtu, dtd, dtv = [part(256, 4608 if i == 0 else None) for i in range(5)]
        kT = part(1536, 0).rearrange("p (g b n) -> p g b n", g=4, b=3)
        vA = part(1536).rearrange("p (b n) -> p b n", b=3)
        qt = part(1024).rearrange("p (s n) -> p s n", s=2)
        qT = part(1024).rearrange("p (s h n) -> p s h n", s=2, h=4)
        Pc = part(512).rearrange("p (h n) -> p h n", h=4)
        Pl = part(1024).rearrange("p (h n) -> p h n", h=4)
        kraw = Pc.rearrange("p h n -> p (h n)")
        PT = part(1536).rearrange("p (b n) -> p b n", b=3)
        rtmp = PT[:, 0]
        zaT = part(1024)
        vg = part(384).rearrange("p (b n) -> p b n", b=3)
        sg = part(1024, 8704).rearrange("p (s n) -> p s n", s=2)
        m32 = part(1024, 0).rearrange("p (s n) -> p s n", s=2)
        gb = [part(1024, 1024 + 1024 * i).rearrange("p (s n) -> p s n", s=2) for i in range(2)]
        xch = [part(1024, 3072 + 1024 * i).rearrange("p (s n) -> p s n", s=2) for i in range(2)]
        fng = part(2048, 0)

        cst = sb("cst", [P, K_WIDTH])
        ident, Umat, Lmat = cst[:, K_ID:K_ID + P], cst[:, K_U:K_U + P], cst[:, K_L:K_L + P]
        one = cst[0:P, K_U + P - 1:K_U + P]
        neg = sb("neg", [P, 2, P], BF16)
        identb = sb("identb", [P, P], BF16)
        sel = sb("sel", [P, HG], F32R)
        cvec = sb("cvec", [P, 2, KT])
        csil = sb("csil", [P, 2, KT])
        cond = sb("cond", [P, KT, 4], F32R)
        chw = sb("chw", [P, 320])
        ng = sb("ng", [P, KT])
        arow = sb("arow", [P, 2 * NH])
        dtb = sb("dtb", [P, 2 * NH])
        sink = sb("sink", [P, N_Q])
        mcol = sb("mcol", [P, 2, 2, KT])
        SA = sb("SA", [P, NQ, NH])
        gs = sb("gs", [P, NQ, HG])
        dAg = sb("dAg", [P, 4, P])
        cw = [sb(f"cw{i}", [P, 6, 4]) for i in range(2)]
        nrm = [sb(f"nrm{i}", [P, 4]) for i in range(2)]
        H = sb("H", [P, 2, 2, P], F32R)
        half_exp = sb("half_exp", [P, 2])
        ss = sb("ss", [P, 2])
        rstd = sb("rstd", [P, 2])
        sm = sb("sm", [P, 6, 8])

        PM = ctx.enter_context(nc.psum_tensor("PM", [P, 4, 512], F32))
        A = ctx.enter_context(nc.psum_tensor("A", [P, 4, 512], F32))

        raw_loaded = [sem(f"raw_loaded{i}") for i in range(4)]
        hi_ready = sem("hi_ready")
        lo_ready = sem("lo_ready")
        w_used = sem("w_used")
        bank_free = [sem("bank_free0"), sem("bank_free1")]
        phase_done = {e: sem(f"phase_done_{e}") for e in ("pe", "act", "dve", "pool")}
        wait_passed = sem("wait_passed")
        act_chain, dve_chain, pool_chain = sem("act_chain"), sem("dve_chain"), sem("pool_chain")
        S = {}

        def s_(name):
            if name not in S:
                S[name] = sem(name)
            return S[name]

        me = [None]
        DMA = 16
        CR = 4
        ONE = 1
        START_AT_ONE = {
            "pe": ("y_part", "mod_sum", "q_T", "scores_done", "p_T", "o_done", "m_T"),
            "act": ("st_stored", "PT_ready", "conv_silu", "xt_ready"),
            "dve": ("yT_read", "a_read", "mT_ready", "sg_used", "aT_ready", "conv_done", "xnew"),
            "pool": ("ST_free", "modfin_free"),
        }

        def start_at_one(eng):
            for name in START_AT_ONE[me[0]]:
                eng.sem_inc(s_(name), ONE)

        block = ctx.enter_context(nc.Block())

        def load_half(sp, c, i, src):
            sp.wait_ge(lo_ready, 8 * c + i + 1)
            n = src.shape[-1]
            sp.dma_start(raw[:, i % 4, :, 0:n], src).then_inc(raw_loaded[i % 4], DMA)

        def hi_half(act, c, i, n=N):
            act.wait_ge(raw_loaded[i % 4], (2 * c + i // 4 + 1) * DMA)
            act.wait_ge(w_used, 8 * c + i + 1)
            act.activation(w_h[:, i % 4, :, 0:n], raw[:, i % 4, :, 0:n], ACT.Copy).then_inc(hi_ready, 1)

        def lo_half(dve, c, i, n=N):
            dve.wait_ge(hi_ready, 8 * c + i + 1)
            dve.tensor_tensor(w_l[:, i % 4, :, 0:n], raw[:, i % 4, :, 0:n],
                              w_h[:, i % 4, :, 0:n].bitcast(F32), ALU.subtract).then_inc(lo_ready, 1)

        def mm_half(pe, c, i, kind, par, hi=None, lo=None, last=7, n=N):
            pe.wait_ge(lo_ready, 8 * c + i + 1 + CR)
            mm = None
            for kk in range(2):
                kt = 2 * i + kk
                st, en = kt == 0, kt == 2 * last + 1
                wh, wl = w_h[:, i % 4, kk, 0:n], w_l[:, i % 4, kk, 0:n]
                if kind == "tok":
                    for s in range(2):
                        out = PM[:, 2 * par + s, 0:n] if n == N else A[:, 0, s * n:(s + 1) * n]
                        tk = slice(s * TOK, (s + 1) * TOK)
                        bank_first = st and (n == N or s == 0)
                        pe.matmul(out, hi[:, kt, tk], wh, start=bank_first, stop=False, skip_group_check=True)
                        pe.matmul(out, hi[:, kt, tk], wl, start=False, stop=False, skip_group_check=True)
                        mm = pe.matmul(out, lo[:, kt, tk], wh, start=False, stop=en, skip_group_check=True)
                elif kind == "ch":
                    for t in range(4):
                        out = PM[:, 2 * par + t // 2, (t % 2) * 256:(t % 2 + 1) * 256]
                        cs = slice(t * P, (t + 1) * P)
                        pe.matmul(out, wh[:, cs], hi[:, kt], start=st and t % 2 == 0, stop=False, skip_group_check=True)
                        pe.matmul(out, wh[:, cs], lo[:, kt], start=False, stop=False, skip_group_check=True)
                        mm = pe.matmul(out, wl[:, cs], hi[:, kt], start=False, stop=en, skip_group_check=True)
                else:
                    out = PM[0:4, 2 * par]
                    pe.matmul(out, cond[:, kt], wh, start=st, stop=False, skip_group_check=True)
                    mm = pe.matmul(out, cond[:, kt], wl, start=False, stop=en, skip_group_check=True)
            mm.then_inc(w_used, 1)

        def bank_wait(pe, par, use):
            pe.wait_ge(bank_free[par], use + 1)

        def chunk_done(eng, c, n=8):
            eng.wait_ge(w_used, 8 * c + n + CR)

        def wait_alone(eng, semaphore, value):
            eng.wait_ge(semaphore, value)
            eng.sem_inc(wait_passed, 1)

        def end_phase(eng):
            eng.drain().then_inc(phase_done[me[0]], 1)

        def after_phase(eng, L, idx):
            for e, semaphore in phase_done.items():
                if e != me[0]:
                    wait_alone(eng, semaphore, L * PHASES + idx + 1)

        def span(start, n):
            return slice(start, start + n) if isinstance(start, int) else bass.ds(start, n)

        def psum_sub(par, t):
            return PM[:, 2 * par + t // 2, (t % 2) * 256:(t % 2 + 1) * 256].rearrange("p (s n) -> p s n", s=2)

        @block.sync
        def _(sp):
            def cols(w, L, c0, kt0=0, n=N, natural=False):
                v = w[L].rearrange("(k p) n -> p k n", p=P) if natural else w[L].rearrange("(p k) n -> p k n", p=P)
                return v[:, kt0:kt0 + 2, span(c0, n)]

            def chunk(L, c, w, c0, halves=8, n=N, natural=False):
                for i in range(halves):
                    load_half(sp, c, i, cols(w, L, c0, 2 * i, n, natural))

            with sp.Fori(0, DEPTH) as L:
                base = L * CHUNKS
                with sp.Fori(0, NMOD) as j:
                    chunk(L, base + PH_MOD + j, a["w_mod"], j * N)
                chunk(L, base + PH_DT, a["w_in"], C_DT, n=2 * NH)
                with sp.Fori(0, 4) as j:
                    chunk(L, base + PH_BC + j, a["w_in"], j * N + C_BC)
                with sp.Fori(0, NG) as g:
                    chunk(L, base + PH_SSD + g * 2, a["w_in"], g * N + C_XBC)
                    chunk(L, base + PH_SSD + g * 2 + 1, a["w_in"], g * N + C_ZS)
                with sp.Fori(0, 4) as j:
                    chunk(L, base + PH_PS + j * 3, a["w_in"], j * N + C_GS)
                    chunk(L, base + PH_PS + j * 3 + 1, a["w_ps"], j * N, halves=16, natural=True)
                chunk(L, base + PH_KV, a["w_in"], C_K)
                chunk(L, base + PH_KV + 1, a["w_in"], C_V)
                with sp.Fori(0, 4) as g:
                    chunk(L, base + PH_Q + g * 2, a["w_in"], g * N + C_Q)
                    chunk(L, base + PH_Q + g * 2 + 1, a["w_in"], g * N + C_ZA)
                with sp.Fori(0, 4) as j:
                    chunk(L, base + PH_PA + j * 2, a["w_in"], j * N + C_GA)
                    chunk(L, base + PH_PA + j * 2 + 1, a["w_pa"], j * N, natural=True)
                with sp.Fori(0, 4) as j:
                    chunk(L, base + PH_OUT + j, a["w_out"], j * N, natural=True)

        @block.tensor
        def _(pe):
            me[0] = "pe"
            start_at_one(pe)
            pe.sem_inc(w_used, CR)

            def halves(c, kind, par, use, hi, lo, steps, first=0, n_halves=8):
                bank_wait(pe, par, use)
                for i in range(n_halves):
                    mm_half(pe, c, i, kind, par, hi, lo, last=n_halves - 1)
                    for step in steps.get(first + i, ()):
                        step()

            def transpose(out, in_):
                return pe.transpose(out, in_, ident[0:in_.shape[0], 0:in_.shape[0]])

            def fp32(out, lhsT, rhs, start, stop=True):
                return pe.matmul(out, lhsT, rhs, start=start, stop=stop, skip_group_check=True)

            pe.wait_ge(s_("cond_ready"), 1)
            pe.wait_ge(s_("const_loaded"), DMA)
            pe.wait_ge(s_("const_cast"), 1)
            end_phase(pe)
            with pe.Fori(0, DEPTH) as L:
                base, ub = L * CHUNKS, L * USES
                after_phase(pe, L, 0)
                pe.wait_ge(s_("rows_loaded"), L * (4 * DMA) + 4 * DMA)
                transpose(A[:, 3, 0:120], rows[0:120, 0])
                transpose(A[:, 3, 120:240], rows[0:120, 1])
                transpose(A[:, 3, 240:320], rows[0:80, 2]).then_inc(s_("rows_T"), 1)
                with pe.Fori(0, NMOD // 2) as j:
                    for par in range(2):
                        def combine(par=par):
                            pe.wait_ge(s_("modrow_ready"), L * NMOD + j * 2 + par + 1)
                            pe.wait_ge(s_("modbias_loaded"), (L * NMOD + j * 2 + par + 1) * DMA)
                            wait_alone(pe, s_("modfin_ready"), L * NMOD + j * 2 + par + 1)
                            fp32(A[0:2, par], cst[0:5, K_COMB:K_COMB + 2], modrow[par][0:5, :], True)\
                                .then_inc(s_("mod_sum"), 1)
                        halves(base + PH_MOD + j * 2 + par, "mod", par, ub + U_MOD + j, None, None, {7: [combine]})
                end_phase(pe)
                after_phase(pe, L, 1)
                for q in range(4):
                    if q == 0:
                        pe.wait_ge(s_("xn_ready"), L + 1)
                    if q >= 2:
                        pe.wait_ge(s_("h32_ready"), L * 4 + q - 1)
                    for t in range(4):
                        for s in range(2):
                            v = x2[:, s, :].rearrange("p (c k) -> p k c", k=KT)[:, 4 * q + t, :]
                            mm = transpose(A[:, 2 * (q % 2) + t // 2, (t % 2) * 256 + s * P:(t % 2) * 256 + (s + 1) * P], v)
                    mm.then_inc(s_("xn_T"), 1)
                for i in range(8):
                    if i % 2 == 0:
                        pe.wait_ge(s_("hT_ready"), L * 4 + i // 2 + 1)
                    if i == 0:
                        pe.wait_ge(s_("h32_ready"), L * 4 + 4)
                    mm_half(pe, base + PH_DT, i, "tok", 0, hT_h, hT_l, n=2 * NH)
                end_phase(pe)

                def log_decays():
                    pe.wait_ge(s_("dA_ready"), L + 1)
                    fp32(A[:, 1, 0:256].rearrange("p (d s n) -> p d s n", d=2, s=2)[:, 0], Umat, SA[:, 8:10, :], True)
                    fp32(A[:, 1, 0:256].rearrange("p (d s n) -> p d s n", d=2, s=2)[:, 1], Lmat, SA[:, 10:12, :], False)
                    fp32(A[:, 1, 256:384].rearrange("p (d n) -> p d n", d=2), one.to_broadcast([P, P]),
                         SA[:, 8:12:2, :], False).then_inc(s_("acs_ready"), 1)
                with pe.Fori(0, 2) as j:
                    halves(base + PH_BC + j * 2, "ch", 0, ub + U_BC + j, hT_h, hT_l, {})
                    halves(base + PH_BC + j * 2 + 1, "ch", 1, ub + U_BC + j, hT_h, hT_l, {})
                log_decays()
                end_phase(pe)

                def ssd_steps(q):
                    G = L * NG + q

                    def start():
                        pe.wait_ge(s_("group_copied"), G + 1)
                        pe.wait_ge(s_("st_stored"), G + ONE)
                        for s in range(2):
                            fp32(A[:, 2, s * P:(s + 1) * P], BCg[:, 0, s * P:(s + 1) * P], BCg[:, 1, s * P:(s + 1) * P], s == 0)
                        fp32(A[:, 2, 256:384], BCg[:, 0, 0:P], ident, False).then_inc(s_("cb_done"), 1)
                        for ds in range(4):
                            mm = fp32(A[:, 3, ds * P:(ds + 1) * P], dAg[:, ds], (Umat, Lmat)[ds // 2], ds == 0)
                        mm.then_inc(s_("acsT_done"), 1)

                    def states_T():
                        pe.wait_ge(s_("xt_ready"), G + 1 + ONE)
                        pe.wait_ge(s_("st_loaded"), (G + 1) * 2 * DMA)
                        for d in range(2):
                            for t in range(4):
                                mm = transpose(A[:, d, t * P:(t + 1) * P], stload[:, d, t])
                        mm.then_inc(s_("stT_done"), 1)

                    def decay(h):
                        if h == 0:
                            pe.wait_ge(s_("H_ready"), G + 1)
                            pe.wait_ge(s_("cb_ready"), G + 1)
                            pe.wait_ge(s_("bt_ready"), G + 1)
                        if h >= 2:
                            pe.wait_ge(s_("exp_done"), G * HG + h - 1)
                        b = A[:, 2 + h % 2, :]
                        pe.matmul(b, sel[:, h:h + 1].to_broadcast([P, P]), H[:].rearrange("p d s n -> p (d s n)"),
                                  start=True, stop=False, skip_group_check=True)
                        mm = None
                        for d in range(2):
                            mm = pe.matmul(b[:, d * 256:(d + 1) * 256].rearrange("p (s n) -> p s n", s=2), identb[:],
                                           neg[:, d:d + 1, :].to_broadcast([P, 2, P]), start=False, stop=True,
                                           skip_group_check=True)
                        mm.then_inc(s_("decay_done"), 1)

                    def y_diag(h):
                        if h == 0:
                            pe.wait_ge(s_("ST_ready"), G + 1)
                        pe.wait_ge(s_("M_ready"), G * HG + h + 1)
                        for s in range(2):
                            for d in range(2):
                                mm = fp32(A[:, s, h * HP:(h + 1) * HP], E[h % 2][:, d, s, :], xt[:, s, h * HP:(h + 1) * HP],
                                          h == 0 and d == 0, stop=(d == 1))
                        mm.then_inc(s_("y_part"), 1)

                    def y_start():
                        pe.wait_ge(s_("exp_done"), G * HG + HG)
                        for d in range(2):
                            mm = fp32(A[:, 2 + d, :], BCg[:, 1, P:256], ST[:, d, :], True)
                        mm.then_inc(s_("yoff_done"), 1)

                    def final_states():
                        pe.wait_ge(s_("yoff_read"), G + 1)
                        pe.wait_ge(s_("xw_ready"), G + 1)
                        for d in range(2):
                            for t in range(4):
                                mm = fp32(A[:, 2 + d, t * P:(t + 1) * P], xw[:, d, t * P:(t + 1) * P], Bt, t == 0)
                        mm.then_inc(s_("stf_done"), 1)

                    def y_T():
                        pe.wait_ge(s_("yn_ready"), G + 1)
                        for t in range(4):
                            for s in range(2):
                                mm = transpose(A[:, t // 2, (t % 2) * 256 + s * P:(t % 2) * 256 + (s + 1) * P],
                                               y[:, s, t * P:(t + 1) * P])
                        mm.then_inc(s_("yT_done"), 1)

                    st = {0: [start], 1: [states_T], 13: [y_start, final_states], 14: [y_T]}
                    for h in range(HG):
                        st.setdefault(max(2, 2 + h), []).append(lambda h=h: decay(h))
                        st.setdefault(4 + h, []).append(lambda h=h: y_diag(h))
                    return st

                def xt_T(g):
                    pe.wait_ge(s_("xc_ready"), L * NG + g + 1)
                    pe.wait_ge(s_("yT_read"), L * NG + g + ONE)
                    for s in range(2):
                        for t in range(4):
                            mm = transpose(A[:, s, t * P:(t + 1) * P], xc[:, t * 256 + s * P:t * 256 + (s + 1) * P])
                    mm.then_inc(s_("xt_T"), 1)

                def ssd_body(g, steps):
                    st = dict(steps)
                    st[15] = list(st.get(15, ())) + [lambda: xt_T(g)]
                    halves(base + PH_SSD + g * 2, "ch", 0, ub + U_SSD + g, hT_h, hT_l, st)
                    halves(base + PH_SSD + g * 2 + 1, "tok", 1, ub + U_SSD + g, hT_h, hT_l, st, first=8)

                after_phase(pe, L, 3)
                ssd_body(0, {})
                with pe.Fori(1, NG) as g:
                    ssd_body(g, ssd_steps(g - 1))
                for i, steps in sorted(ssd_steps(NG - 1).items()):
                    for step in steps:
                        step()
                end_phase(pe)

                wait_alone(pe, s_("yT_read"), L * NG + NG + ONE)
                with pe.Fori(0, 4) as j:
                    halves(base + PH_PS + j * 3, "tok", 0, ub + U_PS + j, hT_h, hT_l, {})
                    halves(base + PH_PS + j * 3 + 1, "tok", 1, ub + U_PS + j, yT_h, yT_l, {}, n_halves=16)
                end_phase(pe)
                after_phase(pe, L, 5)

                def k_T():
                    pe.wait_ge(s_("k_ready"), L + 1)
                    pe.wait_ge(s_("kv_loaded"), (L + 1) * 2 * DMA)
                    for b, src in enumerate((kraw, qt[:, 1], qt[:, 0])):
                        for h in range(N_KV):
                            mm = transpose(A[:, b, h * P:(h + 1) * P], src[:, h * P:(h + 1) * P])
                    mm.then_inc(s_("k_T"), 1)
                halves(base + PH_KV, "tok", 0, ub + U_KV, hT_h, hT_l, {})
                halves(base + PH_KV + 1, "tok", 1, ub + U_KV, hT_h, hT_l, {7: [k_T]})
                end_phase(pe)
                after_phase(pe, L, 6)

                def q_scores(g):
                    G = L * 4 + g
                    pe.wait_ge(s_("q_ready"), G + 1)
                    pe.wait_ge(s_("PT_ready"), G + ONE)
                    for s in range(2):
                        for h in range(4):
                            mm = transpose(A[:, s, h * P:(h + 1) * P], qt[:, s, h * P:(h + 1) * P])
                    mm.then_inc(s_("q_T"), 1)

                def scores(g):
                    G = L * 4 + g
                    pe.wait_ge(s_("qT_ready"), G + 1)
                    pe.wait_ge(s_("a_read"), G + ONE)
                    kTg = kT[:, span(g, 1), :, :].rearrange("p g b n -> p (g b n)")
                    for h in range(4):
                        fp32(A[:, 2, h * P:(h + 1) * P], qT[:, 0, h], kTg[:, 256:384], h == 0)
                    for h in range(4):
                        mm = fp32(A[:, h // 2, (h % 2) * 256:(h % 2 + 1) * 256], qT[:, 1, h], kTg[:, 0:256], h % 2 == 0)
                    mm.then_inc(s_("scores_done"), 1)

                def attn_steps(q):
                    G = L * 4 + q

                    def p_T():
                        pe.wait_ge(s_("p_ready"), G + 1)
                        for h in range(4):
                            transpose(A[:, 0, h * P:(h + 1) * P], Pl[:, h, 0:P])
                            transpose(A[:, 1, h * P:(h + 1) * P], Pl[:, h, P:256])
                            mm = transpose(A[:, 2, h * P:(h + 1) * P], Pc[:, h])
                        mm.then_inc(s_("p_T"), 1)

                    def pv():
                        pe.wait_ge(s_("PT_ready"), G + 1 + ONE)
                        pe.wait_ge(s_("vg_ready"), G + 1)
                        fp32(A[:, 3, :], vg[:, 2], PT[:, 2], True)
                        fp32(A[:, 2, :], vg[:, 0], PT[:, 0], True, stop=False)
                        fp32(A[:, 2, :], vg[:, 1], PT[:, 1], False).then_inc(s_("o_done"), 1)
                    return {0: [p_T], 3: [pv]}

                def q_body(g, steps):
                    st = dict(steps)
                    st[12] = [lambda: q_scores(g)]
                    st[14] = [lambda: scores(g)]
                    halves(base + PH_Q + g * 2, "tok", 0, ub + U_Q + g, hT_h, hT_l, st)
                    halves(base + PH_Q + g * 2 + 1, "ch", 1, ub + U_Q + g, hT_h, hT_l, st, first=8)
                q_body(0, {})
                with pe.Fori(1, 4) as g:
                    q_body(g, attn_steps(g - 1))
                for i, steps in sorted(attn_steps(3).items()):
                    for step in steps:
                        step()
                end_phase(pe)

                pe.wait_ge(s_("aT_ready"), L * 4 + 4 + ONE)

                def m_T(q):
                    pe.wait_ge(s_("m_ready"), L * 4 + q + 1)
                    pe.wait_ge(s_("mT_ready"), L * 4 + q + ONE)
                    for t in range(4):
                        for s in range(2):
                            mm = transpose(A[:, t // 2, (t % 2) * 256 + s * P:(t % 2) * 256 + (s + 1) * P],
                                           m32[:, s, t * P:(t + 1) * P])
                    mm.then_inc(s_("m_T"), 1)

                def pa_body(j, steps):
                    halves(base + PH_PA + j * 2, "tok", 0, ub + U_PA + j, hT_h, hT_l, steps)
                    halves(base + PH_PA + j * 2 + 1, "tok", 1, ub + U_PA + j, aT_h, aT_l, {})
                pa_body(0, {})
                with pe.Fori(1, 4) as j:
                    pa_body(j, {5: [lambda: m_T(j - 1)]})
                m_T(3)
                end_phase(pe)

                wait_alone(pe, s_("mT_ready"), L * 4 + 4 + ONE)
                with pe.Fori(0, 2) as j:
                    halves(base + PH_OUT + j * 2, "tok", 0, ub + U_OUT + j, mT_h, mT_l, {})
                    halves(base + PH_OUT + j * 2 + 1, "tok", 1, ub + U_OUT + j, mT_h, mT_l, {})
                end_phase(pe)

        @block.scalar
        def _(act):
            me[0] = "act"
            start_at_one(act)
            ch = Chain(act, act_chain)
            F = ACT

            def halves(c, steps, first=0, n_halves=8, n=N):
                for i in range(n_halves):
                    hi_half(act, c, i, n)
                    for step in steps.get(first + i, ()):
                        step()

            act.wait_ge(s_("const_loaded"), DMA)
            act.activation(neg[:], cst[:, K_NEG:K_NEG + 2 * P].rearrange("p (d n) -> p d n", d=2), F.Copy)
            act.activation(identb[:], ident, F.Copy)
            act.activation(sel[:], cst[:, K_SEL:K_SEL + HG], F.Copy).then_inc(s_("const_cast"), 1)
            act.wait_ge(s_("cvec_loaded"), 2 * DMA)
            ch.link(act.activation(csil[:], cvec[:], F.Silu))
            ch.wait()
            act.activation(cond[:, :, 0:2].rearrange("p k s -> p s k"), csil[:], F.Copy).then_inc(s_("cond_hi"), 1)
            ch.reset()
            end_phase(act)
            with act.Fori(0, DEPTH) as L:
                base = L * CHUNKS
                after_phase(act, L, 0)
                act.wait_ge(s_("rows_T"), L + 1)
                act.activation(chw[:], A[:, 3, 0:320], F.Copy).then_inc(s_("chw_ready"), 1)
                act.wait_ge(s_("small_loaded"), (L + 1) * 6 * DMA)
                act.activation(arow[:], arow[:], F.Exp).then_inc(s_("arow_exp"), 1)
                act.wait_ge(s_("x_ready"), L + 1)
                for s in range(2):
                    if s:
                        ch.wait()
                    ch.link(act.activation(sq_dump, x2[:, s], F.Square, accum_out=ss[:, s:s + 1]))
                ch.wait()
                act.activation(sm[:, 0, 0:2], ss[:], F.Copy).then_inc(s_("ss_ready"), 1)
                ch.reset()
                with act.Fori(0, NMOD // 2) as j:
                    for par in range(2):
                        def evac(par=par):
                            chunk_done(act, base + PH_MOD + j * 2 + par)
                            act.wait_ge(s_("mod_sum"), L * NMOD + j * 2 + par + ONE)
                            act.activation(modrow[par][0:4, :], PM[0:4, 2 * par], F.Copy).then_inc(s_("modrow_ready"), 1)
                        halves(base + PH_MOD + j * 2 + par, {7: [evac]})
                end_phase(act)

                def h_hi(q):
                    act.wait_ge(s_("h32_ready"), L * 4 + q + 1)
                    act.activation(hT_h[:, 4 * q:4 * q + 4].rearrange("p k n -> p (k n)"), h32[q % 2], F.Copy)\
                        .then_inc(s_("hT_hi"), 1)
                for q in range(4):
                    h_hi(q)
                halves(base + PH_DT, {}, n=2 * NH)
                act.wait_ge(s_("dt_abs"), L + 1)
                act.activation(dte, dtd, F.Exp, scale=-1.0).then_inc(s_("dt_exp"), 1)
                act.wait_ge(s_("dt_u"), L + 1)
                act.activation(dtv, dtu, F.Ln).then_inc(s_("dt_ln"), 1)
                end_phase(act)

                with act.Fori(0, 2) as j:
                    def conv(par):
                        k = L * 4 + j * 2 + par
                        chunk_done(act, base + PH_BC + j * 2 + par)
                        dst = BC[:, bass.ds(j * 8 + 4 * par, 4), :]
                        act.wait_ge(s_("cw_copied"), L * 12 + j * 2 + par + 1)
                        act.wait_ge(s_("conv_silu"), L * 12 + j * 2 + par + ONE)
                        for t in range(4):
                            mm = act.activation(xc[:, t * 256:(t + 1) * 256].rearrange("p (s n) -> p s n", s=2),
                                                psum_sub(par, t), F.Identity,
                                                bias=cw[par][:, 5, t:t + 1], scale=cw[par][:, 2, t:t + 1])
                        mm.then_inc(s_("conv_center"), 1)

                    def silu(par):
                        act.wait_ge(s_("conv_done"), L * 12 + j * 2 + par + 1 + ONE)
                        act.activation(BC[:, bass.ds(j * 8 + 4 * par, 4), :].rearrange("p t n -> p (t n)"), xc, F.Silu)\
                            .then_inc(s_("conv_silu"), 1)
                    halves(base + PH_BC + j * 2, {})
                    halves(base + PH_BC + j * 2 + 1, {3: [lambda: conv(0)], 6: [lambda: silu(0)], 7: [lambda: conv(1), lambda: silu(1)]})
                act.wait_ge(s_("tail_ready"), L + 1)
                act.activation(SA[:, 14:16, :], SA[:, 1:4:2, :], F.Exp, scale=-1.0)
                act.activation(SA[:, 12:14, :], SA[:, 12:14, :], F.Exp).then_inc(s_("ew_exp"), 1)
                end_phase(act)

                def ssd_steps(q):
                    G = L * NG + q

                    def evacs():
                        act.wait_ge(s_("xt_T"), G + 1)
                        act.activation(xt[:], A[:, 0:2, :], F.Copy).then_inc(s_("xt_ready"), 1)
                        chunk_done(act, base + PH_SSD + q * 2 + 1)
                        act.activation(zs[:], PM[:, 2:4, :], F.Silu).then_inc(bank_free[1], 1)

                    def H_hi():
                        act.wait_ge(s_("acsT_done"), G + 1)
                        act.activation(H[:].rearrange("p d s n -> p (d s n)"), A[:, 3, :], F.Copy).then_inc(s_("H_hi"), 1)
                        act.wait_ge(s_("cb_ready"), G + 1)
                        act.activation(Bt, A[:, 2, 256:384], F.Copy).then_inc(s_("bt_ready"), 1)

                    def ST_copy():
                        act.wait_ge(s_("stT_done"), G + 1)
                        act.wait_ge(s_("ST_free"), G + ONE)
                        act.activation(ST[:], A[:, 0:2, :], F.Copy).then_inc(s_("ST_ready"), 1)

                    def exp(h):
                        act.wait_ge(s_("decay_done"), G * HG + h + 1)
                        if h >= 2:
                            act.wait_ge(s_("y_part"), G * HG + h - 1 + ONE)
                        for d in range(2):
                            for s in range(2):
                                mm = act.activation(E[h % 2][:, d, s, :], A[:, 2 + h % 2, (2 * d + s) * P:(2 * d + s + 1) * P],
                                                    F.Exp, bias=gs[:, 2 * d + s, h:h + 1])
                        mm.then_inc(s_("exp_done"), 1)

                    def stores():
                        act.wait_ge(s_("stf_done"), G + 1)
                        act.activation(ST[:], A[:, 2:4, :], F.Copy).then_inc(s_("st_stored"), 1)

                    def squares():
                        act.wait_ge(s_("yz_ready"), G + 1)
                        for s in range(2):
                            if s:
                                ch.wait()
                            ch.link(act.activation(xw[:, 0], y[:, s], F.Square, accum_out=ss[:, s:s + 1]))
                        ch.wait()
                        act.activation(sm[:, 0, 0:2], ss[:], F.Copy).then_inc(s_("yss_ready"), 1)

                    def y_hi():
                        act.wait_ge(s_("yT_done"), G + 1)
                        act.wait_ge(s_("nrm_copied"), G + 1)
                        for t in range(4):
                            mm = act.activation(yT_h[:, span(q * 4 + t, 1), :],
                                                A[:, t // 2:t // 2 + 1, (t % 2) * 256:(t % 2 + 1) * 256], F.Copy,
                                                scale=nrm[0][:, t:t + 1])
                        mm.then_inc(s_("y_hi"), 1)
                    st = {2: [evacs], 3: [H_hi], 4: [ST_copy], 13: [stores], 14: [squares]}
                    for h in range(HG):
                        st.setdefault(4 + h, []).append(lambda h=h: exp(h))
                    st[15] = [y_hi]
                    return st

                def conv(g):
                    chunk_done(act, base + PH_SSD + g * 2)
                    act.wait_ge(s_("cw_copied"), L * 12 + 4 + g + 1)
                    act.wait_ge(s_("conv_silu"), L * 12 + 4 + g + ONE)
                    act.wait_ge(s_("xt_ready"), L * NG + g + ONE)
                    for t in range(4):
                        mm = act.activation(xc[:, t * 256:(t + 1) * 256].rearrange("p (s n) -> p s n", s=2),
                                            psum_sub(0, t), F.Identity,
                                            bias=cw[0][:, 5, t:t + 1], scale=cw[0][:, 2, t:t + 1])
                    mm.then_inc(s_("conv_center"), 1)

                def silu(g):
                    act.wait_ge(s_("conv_done"), L * 12 + 4 + g + 1 + ONE)
                    ins = act.activation(xc, xc, F.Silu)
                    ins.then_inc(s_("xc_ready"), 1)
                    act.wait_ge(s_("xc_ready"), L * NG + g + 1)
                    act.sem_inc(s_("conv_silu"), 1)

                def ssd_body(g, steps):
                    st = {k: list(v) for k, v in steps.items()}
                    st[11] = [lambda: conv(g)] + st.get(11, [])
                    st[15] = [lambda: silu(g)] + st.get(15, [])
                    halves(base + PH_SSD + g * 2, st)
                    halves(base + PH_SSD + g * 2 + 1, st, first=8)
                    ch.reset()
                ssd_body(0, {})
                with act.Fori(1, NG) as g:
                    ssd_body(g, ssd_steps(g - 1))
                for i, steps in sorted(ssd_steps(NG - 1).items()):
                    for step in steps:
                        step()
                ch.reset()
                end_phase(act)

                def sigmoid(c, use):
                    chunk_done(act, c)
                    act.wait_ge(s_("sg_used"), L * 8 + use + ONE)
                    act.activation(sg[:], PM[:, 0:2, :], F.Sigmoid).then_inc(s_("sg_ready"), 1)
                    act.wait_ge(s_("sg_ready"), L * 8 + use + 1)
                    act.sem_inc(bank_free[0], 1)
                with act.Fori(0, 4) as j:
                    halves(base + PH_PS + j * 3, {})
                    halves(base + PH_PS + j * 3 + 1, {3: [lambda: after_phase(act, L, 4), lambda: sigmoid(base + PH_PS + j * 3, j)]}, n_halves=16)
                end_phase(act)

                def k_evac():
                    after_phase(act, L, 5)
                    chunk_done(act, base + PH_KV)
                    act.activation(qt[:, 0], PM[:, 0], F.Copy).then_inc(s_("kc_ready"), 1)

                def kT_evac():
                    act.wait_ge(s_("k_T"), L + 1)
                    act.activation(kT[:].rearrange("p g b n -> p b g n"),
                                   A[:, 0:3, :].rearrange("p b (g n) -> p b g n", g=4), F.Copy).then_inc(s_("kT_ready"), 1)
                    chunk_done(act, base + PH_KV + 1)
                    act.wait_ge(s_("kv_loaded"), (L + 1) * 2 * DMA)
                    act.activation(vA[:, 2], PM[:, 2], F.Copy)
                    act.activation(vA[:, 1], PM[:, 3], F.Copy).then_inc(bank_free[1], 1)
                halves(base + PH_KV, {})
                halves(base + PH_KV + 1, {3: [k_evac], 7: [kT_evac]})
                end_phase(act)

                def q_evac(g):
                    chunk_done(act, base + PH_Q + g * 2)
                    act.wait_ge(s_("q_T"), L * 4 + g + ONE)
                    act.activation(qt[:, 0], PM[:, 0], F.Copy).then_inc(s_("qc_ready"), 1)

                def qT_evac(g):
                    act.wait_ge(s_("q_T"), L * 4 + g + 1 + ONE)
                    act.wait_ge(s_("scores_done"), L * 4 + g + ONE)
                    act.activation(qT[:].rearrange("p s h n -> p s (h n)"), A[:, 0:2, :], F.Copy).then_inc(s_("qT_ready"), 1)

                def soft(g):
                    act.wait_ge(s_("nm_ready"), L * 4 + g + 1)
                    act.wait_ge(s_("p_T"), L * 4 + g + ONE)
                    for h in range(4):
                        act.activation(Pc[:, h], A[:, 2, h * P:(h + 1) * P], F.Exp, bias=sm[:, 1, h:h + 1], scale=SCALE,
                                       accum_out=sm[:, 2, h:h + 1])
                    for h in range(4):
                        act.activation(Pl[:, h], A[:, h // 2, (h % 2) * 256:(h % 2 + 1) * 256], F.Exp,
                                       bias=sm[:, 1, 4 + h:5 + h], scale=SCALE, accum_out=sm[:, 2, 4 + h:5 + h])
                    act.activation(sm[:, 4], sm[:, 3], F.Exp).then_inc(s_("exps_done"), 1)

                def attn_steps(q):
                    G = L * 4 + q

                    def pT_evac():
                        act.wait_ge(s_("p_T"), G + 1 + ONE)
                        act.activation(PT[:], A[:, 0:3, :], F.Copy).then_inc(s_("PT_ready"), 1)
                        chunk_done(act, base + PH_Q + q * 2 + 1)
                        act.wait_ge(s_("aT_ready"), G + ONE)
                        act.activation(zaT, PM[:, 2:4, :].rearrange("p b n -> p (b n)"), F.Silu).then_inc(bank_free[1], 1)

                    def a_hi():
                        act.wait_ge(s_("a_read"), G + 1 + ONE)
                        act.activation(aT_h[:, span(q * 4, 4), :],
                                       zaT.rearrange("p (k n) -> p k n", k=4), F.Copy).then_inc(s_("a_hi"), 1)
                    return {2: [pT_evac], 7: [a_hi]}

                def q_body(g, steps):
                    st = {k: list(v) for k, v in steps.items()}
                    st[11] = [lambda: q_evac(g)]
                    st[13] = [lambda: qT_evac(g)]
                    st[15] = [lambda: soft(g)]
                    halves(base + PH_Q + g * 2, st)
                    halves(base + PH_Q + g * 2 + 1, st, first=8)
                after_phase(act, L, 6)
                q_body(0, {})
                with act.Fori(1, 4) as g:
                    q_body(g, attn_steps(g - 1))
                for i, steps in sorted(attn_steps(3).items()):
                    for step in steps:
                        step()
                end_phase(act)

                def m_hi(q):
                    act.wait_ge(s_("m_T"), L * 4 + q + 1 + ONE)
                    act.activation(mT_h[:, span(q * 4, 4), :],
                                   A[:, 0:2, :].rearrange("p b (k n) -> p (b k) n", k=2), F.Copy).then_inc(s_("m_hi"), 1)

                def pa_body(j, steps):
                    halves(base + PH_PA + j * 2, steps)
                    halves(base + PH_PA + j * 2 + 1, {3: [lambda: after_phase(act, L, 7), lambda: sigmoid(base + PH_PA + j * 2, j + 4)]})
                pa_body(0, {})
                with act.Fori(1, 4) as j:
                    pa_body(j, {6: [lambda: m_hi(j - 1)]})
                m_hi(3)
                end_phase(act)
                with act.Fori(0, 4) as j:
                    halves(base + PH_OUT + j, {})
                end_phase(act)

            after_phase(act, DEPTH, 0)
            for s in range(2):
                if s:
                    ch.wait()
                ch.link(act.activation(arena[:, 2048:4096], x2[:, s], F.Square, accum_out=ss[:, s:s + 1]))
            ch.wait()
            act.activation(sm[:, 0, 0:2], ss[:], F.Copy).then_inc(s_("ss_ready"), 1)

        @block.vector
        def _(dve):
            me[0] = "dve"
            start_at_one(dve)
            dve.sem_inc(lo_ready, CR)
            dve.sem_inc(s_("modfin_ready"), 2)
            ch = Chain(dve, dve_chain)

            def halves(c, steps, first=0, n_halves=8, n=N):
                for i in range(n_halves):
                    lo_half(dve, c, i, n)
                    for step in steps.get(first + i, ()):
                        step()

            def tt(out, a_, b_, op):
                return dve.tensor_tensor(out, a_, b_, op)

            dve.sem_inc(bank_free[0], 1)
            dve.sem_inc(bank_free[1], 1)
            dve.memset(half_exp[:], -0.5).then_inc(s_("half_exp_set"), 1)
            dve.wait_ge(s_("cond_hi"), 1)
            tt(cond[:, :, 2:4].rearrange("p k s -> p s k"), csil[:],
               cond[:, :, 0:2].bitcast(F32).rearrange("p k s -> p s k"), ALU.subtract).then_inc(s_("cond_ready"), 1)
            end_phase(dve)

            def rope(src, out):
                x = src.rearrange("p (h c f w) -> p h c f w", h=4, c=2, f=2)
                cos = cst[:, K_COS:K_COS + P].rearrange("p (c f w) -> p c f w", c=2, f=2)
                sin = cst[:, K_SIN:K_SIN + P].rearrange("p (c f w) -> p c f w", c=2, f=2)
                r = rtmp.rearrange("p (h c f w) -> p h c f w", h=4, c=2, f=2)
                ov = out.rearrange("p (h n) -> p h n", h=4)
                tt(ov, src.rearrange("p (h n) -> p h n", h=4),
                   cst[:, K_COS:K_COS + P].unsqueeze(1).to_broadcast([P, 4, P]), ALU.mult)
                for f in range(2):
                    for c in range(2):
                        k = tt(r[:, :, c, f], x[:, :, c, 1 - f],
                               sin[:, c, f].unsqueeze(1).to_broadcast([P, 4, 32]), ALU.mult)
                ch.link(k)
                ch.wait()
                return tt(out, out, rtmp, ALU.add)

            def conv_taps(par, cbuf):
                at = []
                for t in range(4):
                    acc = xc[:, t * 256:(t + 1) * 256].rearrange("p (s n) -> p s n", s=2)
                    at.append((acc, psum_sub(par, t)))
                last = {}
                ins = None
                for j in (0, 1, 3, 4):
                    d = j - 2
                    lo_, hi_ = max(0, -d), TOK - max(0, d)
                    for t, (acc, u) in enumerate(at):
                        if t in last:
                            ch.wait(last[t])
                        o_ = acc[:, :, lo_:hi_]
                        ins = dve.scalar_tensor_tensor(out=o_, in0=u[:, :, lo_ + d:hi_ + d], scalar=cw[cbuf][:, j, t:t + 1],
                                                       in1=o_, op0=ALU.mult, op1=ALU.add)
                        if not (j == 4 and t == 3):
                            last[t] = ch.link(ins)
                ins.then_inc(bank_free[par], 1)

            with dve.Fori(0, DEPTH) as L:
                base, ub = L * CHUNKS, L * USES
                after_phase(dve, L, 0)
                dve.wait_ge(s_("arow_exp"), L + 1)
                dve.tensor_scalar(arow[:], arow[:], -1.0, None, ALU.mult).then_inc(s_("arow_ready"), 1)
                dve.wait_ge(s_("rstd_ready"), L + 1)
                for s in range(2):
                    ins = dve.tensor_scalar(x2[:, s], x2[:, s], rstd[:, s:s + 1], None, ALU.mult)
                ins.then_inc(s_("xn_ready"), 1)
                with dve.Fori(0, NMOD // 2) as j:
                    for par in range(2):
                        def fin(par=par):
                            k = L * NMOD + j * 2 + par
                            dve.wait_ge(s_("modrow_ready"), k + 1)
                            dve.sem_inc(bank_free[par], 1)
                            dve.wait_ge(s_("mod_sum"), k + 1 + ONE)
                            dve.wait_ge(s_("modfin_free"), k + ONE)
                            dve.tensor_copy(modfin[par][0:2, :], A[0:2, par]).then_inc(s_("modfin_ready"), 1)
                        halves(base + PH_MOD + j * 2 + par, {7: [fin]})
                end_phase(dve)
                dve.wait_ge(s_("mcol_loaded"), (L + 1) * 4 * DMA)
                dve.wait_ge(s_("small_loaded"), (L + 1) * 6 * DMA)
                ch.link(dve.scalar_tensor_tensor(out=mcol[:, :, 1, :], in0=mcol[:, :, 1, :], scalar=1.0,
                                                 in1=ng[:].unsqueeze(1).to_broadcast([P, 2, KT]), op0=ALU.add, op1=ALU.mult))
                ch.wait()
                after_phase(dve, L, 1)
                for q in range(4):
                    dve.wait_ge(s_("xn_T"), L * 4 + q + 1)
                    if q >= 2:
                        dve.wait_ge(s_("hT_ready"), L * 4 + q - 1)
                    for t in range(4):
                        for s in range(2):
                            at = t * 256 + s * P
                            kt = 4 * q + t
                            ins = dve.tensor_scalar(h32[q % 2][:, at:at + P],
                                                    A[:, 2 * (q % 2) + t // 2, at % 512:at % 512 + P],
                                                    mcol[:, s, 1, kt:kt + 1], mcol[:, s, 0, kt:kt + 1], ALU.mult, ALU.add)
                    ins.then_inc(s_("h32_ready"), 1)
                    dve.wait_ge(s_("hT_hi"), L * 4 + q + 1)
                    hs = hT_h[:, 4 * q:4 * q + 4].rearrange("p k n -> p (k n)")
                    tt(hT_l[:, 4 * q:4 * q + 4].rearrange("p k n -> p (k n)"), h32[q % 2], hs.bitcast(F32), ALU.subtract)\
                        .then_inc(s_("hT_ready"), 1)
                halves(base + PH_DT, {}, n=2 * NH)
                chunk_done(dve, base + PH_DT)
                z4 = dtz.rearrange("p (s n) -> p s n", s=2)
                ch.link(tt(z4, A[:, 0, 0:256].rearrange("p (s n) -> p s n", s=2),
                           dtb[:].unsqueeze(1).to_broadcast([P, 2, 2 * NH]), ALU.add))
                ch.wait()
                dve.scalar_tensor_tensor(out=dtd, in0=dtz, scalar=-1.0, in1=dtz, op0=ALU.mult, op1=ALU.max).then_inc(s_("dt_abs"), 1)
                dve.wait_ge(s_("dt_exp"), L + 1)
                dve.tensor_scalar(dtu, dte, 1.0, None, ALU.add).then_inc(s_("dt_u"), 1)
                dve.wait_ge(s_("dt_u"), L + 1)
                ch.link(dve.tensor_scalar(dtd, dtu, -1.0, None, ALU.add))
                ch.wait()
                ch.link(tt(dte, dte, dtd, ALU.subtract))
                dve.wait_ge(s_("dt_ln"), L + 1)
                ch.link(dve.reciprocal(dtu, dtu))
                ch.wait()
                ch.link(tt(dte, dte, dtu, ALU.mult))
                ch.link(dve.scalar_tensor_tensor(out=dtz, in0=dtz, scalar=0.0, in1=dtv, op0=ALU.max, op1=ALU.add))
                ch.wait()
                dt_v = SA[:, 4:8, :].rearrange("p (d s) n -> p s d n", d=2)
                ch.link(tt(dt_v, dte.rearrange("p (s d n) -> p s d n", s=2, d=2),
                           dtz.rearrange("p (s d n) -> p s d n", s=2, d=2), ALU.add))
                ch.wait()
                for d in range(2):
                    ins = tt(SA[:, 8 + 2 * d:10 + 2 * d, :], SA[:, 4 + 2 * d:6 + 2 * d, :],
                             arow[:, d * NH:(d + 1) * NH].unsqueeze(1).to_broadcast([P, 2, NH]), ALU.mult)
                ins.then_inc(s_("dA_ready"), 1)
                ch.reset()
                end_phase(dve)

                with dve.Fori(0, 2) as j:
                    def conv(par):
                        dve.wait_ge(s_("conv_center"), L * 12 + j * 2 + par + 1)
                        conv_taps(par, par)
                        dve.wait_ge(bank_free[par], ub + U_BC + j + 2)
                        dve.sem_inc(s_("conv_done"), 1)
                    halves(base + PH_BC + j * 2, {})
                    halves(base + PH_BC + j * 2 + 1, {4: [lambda: conv(0)], 7: [lambda: conv(1)]})
                    ch.reset()
                dve.wait_ge(s_("acs_ready"), L + 1)
                ch.link(dve.tensor_scalar(SA[:, 0:4, :].rearrange("p q n -> p (q n)"), A[:, 1, 0:256], -1.0, None, ALU.mult))
                ch.wait()
                tt(SA[:, 12:14, :], A[:, 1, 256:384].rearrange("p (d n) -> p d n", d=2), SA[:, 0:4:2, :], ALU.add)\
                    .then_inc(s_("tail_ready"), 1)
                dve.wait_ge(s_("ew_exp"), L + 1)
                ch.link(tt(SA[:, 12:14, :], SA[:, 12:14, :], SA[:, 4:8:2, :], ALU.mult))
                ch.reset()
                end_phase(dve)

                def ssd_steps(q):
                    G = L * NG + q

                    def masks():
                        dve.wait_ge(s_("cb_done"), G + 1)
                        dve.wait_ge(s_("y_part"), G * HG + ONE)
                        dve.tensor_copy(CB[:].rearrange("p s n -> p (s n)"), A[:, 2, 0:256]).then_inc(s_("cb_ready"), 1)
                        dve.wait_ge(s_("H_hi"), G + 1)
                        Hl = H[64:128].rearrange("p d s n -> p (d s n)")
                        tt(Hl, A[64:128, 3, :], Hl.bitcast(F32), ALU.subtract).then_inc(s_("H_ready"), 1)

                    def M(h):
                        dve.wait_ge(s_("exp_done"), G * HG + h + 1)
                        if h == 0:
                            dve.wait_ge(s_("cb_ready"), G + 1)
                        for d in range(2):
                            for s in range(2):
                                e = E[h % 2][:, d, s, :]
                                ins = dve.scalar_tensor_tensor(out=e, in0=e, scalar=gs[:, 4 + 2 * d + s, h:h + 1],
                                                               in1=CB[:, s, :], op0=ALU.mult, op1=ALU.mult)
                        ins.then_inc(s_("M_ready"), 1)

                    def add_y():
                        dve.wait_ge(s_("yD_ready"), G + 1)
                        dve.wait_ge(s_("y_part"), G * HG + HG + ONE)
                        ch.link(tt(y[:], y[:], A[:, 0:2, :], ALU.add))
                        dve.wait_ge(s_("yoff_done"), G + 1)
                        for d in range(2):
                            ch.wait()
                            ins = tt(yoff.rearrange("p (h n) -> p h n", h=HG), A[:, 2 + d, :].rearrange("p (h n) -> p h n", h=HG),
                                     gs[:, 14 + d, :].unsqueeze(2).to_broadcast([P, HG, HP]), ALU.mult)
                            if d == 0:
                                ch.link(ins)
                                ch.wait()
                            else:
                                ins.then_inc(s_("yoff_read"), 1)
                                dve.wait_ge(s_("yoff_read"), G + 1)
                            ch.link(tt(y[:, 1], y[:, 1], yoff, ALU.add))
                        ch.wait()
                        tt(y[:], y[:], zs[:], ALU.mult).then_inc(s_("yz_ready"), 1)

                    def scale_y():
                        dve.wait_ge(s_("yrstd_ready"), G + 1)
                        for s in range(2):
                            ins = dve.tensor_scalar(y[:, s], y[:, s], rstd[:, s:s + 1], None, ALU.mult)
                        ins.then_inc(s_("yn_ready"), 1)

                    def y_lo():
                        dve.wait_ge(s_("y_hi"), G + 1)
                        for t in range(4):
                            sl = span(q * 4 + t, 1)
                            ins = dve.scalar_tensor_tensor(out=yT_l[:, sl, :],
                                                           in0=A[:, t // 2:t // 2 + 1, (t % 2) * 256:(t % 2 + 1) * 256],
                                                           scalar=nrm[0][:, t:t + 1], in1=yT_h[:, sl, :].bitcast(F32),
                                                           op0=ALU.mult, op1=ALU.subtract)
                        ins.then_inc(s_("yT_read"), 1)
                    st = {3: [masks], 13: [add_y], 14: [scale_y], 15: [y_lo]}
                    for h in range(HG):
                        st.setdefault(4 + h, []).append(lambda h=h: M(h))
                    return st

                def conv(g):
                    dve.wait_ge(s_("conv_center"), L * 12 + 4 + g + 1)
                    conv_taps(0, 0)
                    dve.wait_ge(bank_free[0], ub + U_SSD + g + 2)
                    dve.sem_inc(s_("conv_done"), 1)

                def ssd_body(g, steps):
                    st = {k: list(v) for k, v in steps.items()}
                    st[12] = [lambda: conv(g)] + st.get(12, [])
                    halves(base + PH_SSD + g * 2, st)
                    halves(base + PH_SSD + g * 2 + 1, st, first=8)
                    ch.reset()
                ssd_body(0, {})
                with dve.Fori(1, NG) as g:
                    ssd_body(g, ssd_steps(g - 1))
                for i, steps in sorted(ssd_steps(NG - 1).items()):
                    for step in steps:
                        step()
                ch.reset()
                end_phase(dve)

                def gate_s(q):
                    chunk_done(dve, base + PH_PS + q * 3 + 1, 16)
                    dve.wait_ge(s_("sg_ready"), L * 8 + q + 1)
                    cs = bass.ds(q * N, N)
                    ins = tt(x2[:, :, cs], PM[:, 2:4, :], sg[:], ALU.mult)
                    ins.then_inc(s_("sg_used"), 1)
                    dve.wait_ge(s_("sg_used"), L * 8 + q + 1 + ONE)
                    dve.sem_inc(bank_free[1], 1)
                with dve.Fori(0, 4) as j:
                    halves(base + PH_PS + j * 3, {})
                    halves(base + PH_PS + j * 3 + 1, {15: [lambda: gate_s(j)]}, n_halves=16)
                end_phase(dve)

                def k_rope():
                    after_phase(dve, L, 5)
                    chunk_done(dve, base + PH_KV)
                    dve.wait_ge(s_("kc_ready"), L + 1)
                    rope(PM[:, 1], qt[:, 1]).then_inc(s_("k_ready"), 1)
                    dve.wait_ge(s_("k_ready"), L + 1)
                    dve.sem_inc(bank_free[0], 1)
                halves(base + PH_KV, {})
                halves(base + PH_KV + 1, {4: [k_rope]})
                ch.reset()
                end_phase(dve)

                def q_rope(g):
                    G = L * 4 + g
                    chunk_done(dve, base + PH_Q + g * 2)
                    dve.wait_ge(s_("qc_ready"), G + 1)
                    dve.wait_ge(s_("q_T"), G + ONE)
                    dve.wait_ge(s_("o_done"), G + ONE)
                    rope(PM[:, 1], qt[:, 1]).then_inc(s_("q_ready"), 1)
                    dve.wait_ge(s_("q_ready"), G + 1)
                    dve.sem_inc(bank_free[0], 1)

                def maxima(g):
                    G = L * 4 + g
                    dve.wait_ge(s_("scores_done"), G + 1 + ONE)
                    dve.tensor_reduce(sm[:, 0, 0:4], A[:, 2, :].rearrange("p (h n) -> p h n", h=4), AX_X, ALU.max)
                    ch.link(dve.tensor_reduce(sm[:, 0, 4:8], A[:, 0:2, :].rearrange("p b (h n) -> p (b h) n", h=2), AX_X, ALU.max))
                    ch.wait()
                    sk = sink[:, span(g * 4, 4)]
                    sk = sk.unsqueeze(1).to_broadcast([P, 2, 4])
                    v = lambda r: sm[:, r].rearrange("p (s h) -> p s h", s=2)
                    ch.link(dve.scalar_tensor_tensor(out=v(1), in0=v(0), scalar=SCALE, in1=sk, op0=ALU.mult, op1=ALU.max))
                    ch.wait()
                    ch.link(dve.tensor_scalar(sm[:, 1], sm[:, 1], -1.0, None, ALU.mult))
                    ch.wait()
                    tt(v(3), v(1), sk, ALU.add).then_inc(s_("nm_ready"), 1)

                def normalize(g):
                    G = L * 4 + g
                    dve.wait_ge(s_("exps_done"), G + 1)
                    ch.link(tt(sm[:, 5], sm[:, 2], sm[:, 4], ALU.add))
                    ch.wait()
                    ch.link(dve.reciprocal(sm[:, 5], sm[:, 5]))
                    ch.wait()
                    tt(Pc[:], Pc[:], sm[:, 5, 0:4].unsqueeze(2).to_broadcast([P, 4, P]), ALU.mult)
                    tt(Pl[:], Pl[:], sm[:, 5, 4:8].unsqueeze(2).to_broadcast([P, 4, 256]), ALU.mult).then_inc(s_("p_ready"), 1)

                def attn_steps(q):
                    G = L * 4 + q

                    def a_mul():
                        dve.wait_ge(s_("o_done"), G + 1 + ONE)
                        dve.wait_ge(bank_free[1], ub + U_Q + q + 2)
                        zv = zaT.rearrange("p (h s n) -> p h s n", h=4, s=2)
                        for s in range(2):
                            ins = tt(zv[:, :, s], A[:, 3 - s, :].rearrange("p (h n) -> p h n", h=4), zv[:, :, s], ALU.mult)
                        ins.then_inc(s_("a_read"), 1)
                        dve.wait_ge(s_("a_hi"), G + 1)
                        sl = span(q * 4, 4)
                        tt(aT_l[:, sl, :], zaT.rearrange("p (k n) -> p k n", k=4), aT_h[:, sl, :].bitcast(F32), ALU.subtract)\
                            .then_inc(s_("aT_ready"), 1)
                    return {7: [a_mul]}

                def q_body(g, steps):
                    st = {k: list(v) for k, v in steps.items()}
                    st[12] = [lambda: q_rope(g)]
                    st[15] = [lambda: maxima(g), lambda: normalize(g)]
                    halves(base + PH_Q + g * 2, st)
                    halves(base + PH_Q + g * 2 + 1, st, first=8)
                    ch.reset()
                after_phase(dve, L, 6)
                q_body(0, {})
                with dve.Fori(1, 4) as g:
                    q_body(g, attn_steps(g - 1))
                for i, steps in sorted(attn_steps(3).items()):
                    for step in steps:
                        step()
                end_phase(dve)

                def merge(q):
                    G = L * 4 + q
                    chunk_done(dve, base + PH_PA + q * 2 + 1)
                    dve.wait_ge(s_("sg_ready"), L * 8 + q + 4 + 1)
                    dve.wait_ge(s_("m_T"), G + ONE)
                    tt(m32[:], PM[:, 2:4, :], sg[:], ALU.mult).then_inc(s_("sg_used"), 1)
                    dve.wait_ge(s_("sg_used"), L * 8 + q + 4 + 1 + ONE)
                    dve.sem_inc(bank_free[1], 1)
                    cs = span(q * N, N)
                    tt(m32[:], m32[:], x2[:, :, cs], ALU.add).then_inc(s_("m_ready"), 1)

                def m_lo(q):
                    dve.wait_ge(s_("m_hi"), L * 4 + q + 1)
                    sl = span(q * 4, 4)
                    tt(mT_l[:, sl, :], A[:, 0:2, :].rearrange("p b (k n) -> p (b k) n", k=2), mT_h[:, sl, :].bitcast(F32),
                       ALU.subtract).then_inc(s_("mT_ready"), 1)

                def pa_body(j, steps):
                    halves(base + PH_PA + j * 2, steps)
                    halves(base + PH_PA + j * 2 + 1, {})
                pa_body(0, {})
                with dve.Fori(1, 4) as j:
                    pa_body(j, {3: [lambda: after_phase(dve, L, 7), lambda: merge(j - 1)], 7: [lambda: m_lo(j - 1)]})
                merge(3)
                m_lo(3)
                end_phase(dve)

                with dve.Fori(0, 2) as j:
                    def resid(par):
                        k = L * 4 + j * 2 + par
                        after_phase(dve, L, 8)
                        chunk_done(dve, base + PH_OUT + j * 2 + par)
                        dve.wait_ge(s_(f"gb_loaded{par}"), (L * 2 + j + 1) * 4 * DMA)
                        tt(gb[par][:], PM[:, 2 * par:2 * par + 2, :], gb[par][:], ALU.mult).then_inc(bank_free[par], 1)
                        dve.wait_ge(bank_free[par], ub + U_OUT + j + 2)
                        tt(x2[:, :, bass.ds(j * (2 * N) + par * N, N)], gb[par][:], xch[par][:], ALU.add).then_inc(s_("xnew"), 1)
                    halves(base + PH_OUT + j * 2, {})
                    halves(base + PH_OUT + j * 2 + 1, {4: [lambda: resid(0)], 7: [lambda: resid(1)]})
                end_phase(dve)

            after_phase(dve, DEPTH, 0)
            dve.wait_ge(s_("rstd_ready"), DEPTH + 1)
            dve.wait_ge(s_("fng_loaded"), DMA)
            for s in range(2):
                ins = dve.scalar_tensor_tensor(out=x2[:, s], in0=x2[:, s], scalar=rstd[:, s:s + 1], in1=fng,
                                               op0=ALU.mult, op1=ALU.mult)
            ins.then_inc(s_("y_final"), 1)

        @block.gpsimd
        def _(pool):
            me[0] = "pool"
            start_at_one(pool)
            ch = Chain(pool, pool_chain)
            ch.link(pool.memset(dAg[:], 0.0))
            ch.wait()
            ch.reset()
            pool.dma_start(cst[:], a["cst"]).then_inc(s_("const_loaded"), DMA)
            for s, v in enumerate((a["c_ctx"], a["c"][0])):
                pool.dma_start(cvec[:, s], v.rearrange("(p k) -> p k", k=KT)).then_inc(s_("cvec_loaded"), DMA)
            for s, v in enumerate((a["x_prompt"][0], a["x_sample"][0])):
                pool.dma_start(x2[:, s], v).then_inc(s_("x_loaded"), DMA)
                pool.dma_start(x_dram[s], v).then_inc(s_("x_copied"), DMA)
            wait_alone(pool, s_("x_loaded"), 2 * DMA)
            wait_alone(pool, s_("x_copied"), 2 * DMA)
            wait_alone(pool, s_("half_exp_set"), 1)
            end_phase(pool)

            def rms(count, width, ready, done):
                wait_alone(pool, s_(ready), count)
                ch.link(pool.tensor_scalar(rstd[:], sm[:, 0, 0:2], 1.0 / width, EPS, ALU.mult, ALU.add))
                ch.wait()
                pool.tensor_tensor(rstd[:], rstd[:], half_exp[:], ALU.pow).then_inc(s_(done), 1)

            with pool.Fori(0, DEPTH) as L:
                base = L * CHUNKS
                after_phase(pool, L, 0)
                pool.sem_inc(s_("x_ready"), 1)
                cv = a["conv_w"][L].rearrange("j (t c) -> (j t) c", c=P)
                pool.dma_start(rows[0:120, 0], cv[0:120, :]).then_inc(s_("rows_loaded"), DMA)
                pool.dma_start(rows[0:120, 1], cv[120:240, :]).then_inc(s_("rows_loaded"), DMA)
                pool.dma_start(rows[0:48, 2], a["conv_b"][L].rearrange("(t c) -> t c", c=P)).then_inc(s_("rows_loaded"), DMA)
                pool.dma_start(rows[48:80, 2], a["ssd_norm_g"][L].rearrange("(t c) -> t c", c=P)).then_inc(s_("rows_loaded"), DMA)

                def bcast(v, n):
                    return v.unsqueeze(0).to_broadcast([P, n])
                for d, (al, db) in enumerate((("a_log_fwd", "dt_bias_fwd"), ("a_log_bwd", "dt_bias_bwd"))):
                    pool.dma_start(arow[:, d * NH:(d + 1) * NH], bcast(a[al][L], NH)).then_inc(s_("small_loaded"), DMA)
                    pool.dma_start(dtb[:, d * NH:(d + 1) * NH], bcast(a[db][L], NH)).then_inc(s_("small_loaded"), DMA)
                pool.dma_start(SA[:, 16, :], bcast(a["d_skip"][L], NH)).then_inc(s_("small_loaded"), DMA)
                pool.dma_start(ng[:], a["norm_g"][L].rearrange("(p k) -> p k", k=KT)).then_inc(s_("small_loaded"), DMA)
                pool.dma_start(sink[:], bcast(a["attn_sink"][L], N_Q)).then_inc(s_("sink_loaded"), DMA)
                rms(L + 1, D_MODEL, "ss_ready", "rstd_ready")
                with pool.Fori(0, NMOD // 2) as j:
                    for par in range(2):
                        k = L * NMOD + j * 2 + par
                        cs = bass.ds(j * (2 * N) + par * N, N)
                        wait_alone(pool, s_("mod_sum"), k + ONE)
                        pool.dma_start(modrow[par][4:5, :], a["b_mod"][L, cs].unsqueeze(0)).then_inc(s_("modbias_loaded"), DMA)
                        wait_alone(pool, s_("modfin_ready"), k + 3)
                        pool.dma_start(mod_dram[:, cs], modfin[par][0:2, :]).then_inc(s_("mod_stored"), DMA)
                        wait_alone(pool, s_("mod_stored"), (k + 1) * DMA)
                        pool.sem_inc(s_("modfin_free"), 1)
                for s in range(2):
                    for w in range(2):
                        pool.dma_start(mcol[:, s, w], mod_dram[s, w * D_MODEL:(w + 1) * D_MODEL].rearrange("(p k) -> p k", k=KT))\
                            .then_inc(s_("mcol_loaded"), DMA)
                ch.reset()
                end_phase(pool)
                end_phase(pool)

                def copy_cw(k, tile, buf):
                    return pool.tensor_copy(cw[buf][:], chw[:, 0:288].rearrange("p (j t) -> p j t", j=6)[:, :, span(tile, 4)])
                wait_alone(pool, s_("chw_ready"), L + 1)
                with pool.Fori(0, 2) as j:
                    for par in range(2):
                        k = L * 12 + j * 2 + par
                        wait_alone(pool, s_("conv_done"), k + ONE)
                        copy_cw(k, j * 8 + 32 + par * 4, par).then_inc(s_("cw_copied"), 1)
                end_phase(pool)
                after_phase(pool, L, 3)

                def ssd_group(q, more):
                    G = L * NG + q
                    for w in range(2):
                        pool.tensor_copy(BCg[:, w:w + 1, :], BC[:, bass.ds(q + 8 * w, 1), :])
                    for w in range(2):
                        pool.tensor_copy(dAg[:, :, 64 * w:64 * w + HG], SA[:, 8:12, span(q * HG, HG)])
                    pool.tensor_copy(gs[:], SA[:, :, span(q * HG, HG)]).then_inc(s_("group_copied"), 1)
                    tiles = span(q * 4 + 288, 4)
                    pool.tensor_copy(nrm[0][:], chw[:, tiles]).then_inc(s_("nrm_copied"), 1)
                    for d, st in enumerate(("state_ssm_fwd", "state_ssm_bwd")):
                        src = a[st][0, L, span(q * HG, HG)].rearrange("h r n -> (h r) n").rearrange("(t p) n -> p t n", p=P)
                        pool.dma_start(stload[:, d], src).then_inc(s_("st_loaded"), DMA)
                    if more:
                        next_cw(q + 1)
                    wait_alone(pool, s_("group_copied"), G + 1)
                    wait_alone(pool, s_("xt_ready"), G + 1 + ONE)
                    hv = "p (h n) -> p h n"
                    for s in range(2):
                        ins = pool.tensor_tensor(y[:, s].rearrange(hv, h=HG), xt[:, s].rearrange(hv, h=HG),
                                                 gs[:, 16, :].unsqueeze(2).to_broadcast([P, HG, HP]), ALU.mult)
                    ins.then_inc(s_("yD_ready"), 1)
                    for d in range(2):
                        ins = pool.tensor_tensor(xw[:, d].rearrange(hv, h=HG), xt[:, 0].rearrange(hv, h=HG),
                                                 gs[:, 12 + d, :].unsqueeze(2).to_broadcast([P, HG, HP]), ALU.mult)
                    ins.then_inc(s_("xw_ready"), 1)
                    wait_alone(pool, s_("st_stored"), G + 1 + ONE)
                    for d, st in enumerate(("state_f_out", "state_b_out")):
                        dst = o[st][0, L, span(q * HG, HG)].rearrange("h r n -> (h r) n").rearrange("(t p) n -> p t n", p=P)
                        pool.dma_start(dst, ST[:, d].rearrange("p (t n) -> p t n", t=4)).then_inc(s_(("st_out", "st_out_b")[d]), DMA)
                    rms(G + 1, SSD_WIDTH // NG, "yss_ready", "yrstd_ready")
                    wait_alone(pool, s_("st_out"), (G + 1) * DMA)
                    wait_alone(pool, s_("st_out_b"), (G + 1) * DMA)
                    pool.sem_inc(s_("ST_free"), 1)
                    wait_alone(pool, s_("yT_read"), G + 1 + ONE)
                    ch.reset()

                def next_cw(g):
                    wait_alone(pool, s_("conv_done"), L * 12 + 4 + g + ONE)
                    copy_cw(g, g * 4, 0).then_inc(s_("cw_copied"), 1)
                next_cw(0)
                with pool.Fori(0, NG - 1) as g:
                    ssd_group(g, True)
                ssd_group(NG - 1, False)
                end_phase(pool)
                end_phase(pool)
                after_phase(pool, L, 5)
                kc = a["cache_k"][0, L].rearrange("t h d -> t (h d)")
                vc = a["cache_v"][0, L].rearrange("t h d -> t (h d)")
                pool.dma_start(kraw, kc).then_inc(s_("kv_loaded"), DMA)
                pool.dma_start(vA[:, 0], vc).then_inc(s_("kv_loaded"), DMA)
                wait_alone(pool, s_("kc_ready"), L + 1)
                pool.dma_start(o["k_out"][0, L].rearrange("t h d -> t (h d)"), qt[:, 0]).then_inc(s_("k_out"), DMA)
                wait_alone(pool, s_("k_out"), (L + 1) * DMA)
                end_phase(pool)
                after_phase(pool, L, 6)
                pool.dma_start(o["v_out"][0, L].rearrange("t h d -> t (h d)"), vA[:, 2]).then_inc(s_("v_out"), DMA)
                with pool.Fori(0, 4) as g:
                    wait_alone(pool, s_("o_done"), L * 4 + g + ONE)
                    pool.tensor_copy(vg[:], vA[:, :, bass.ds(g * P, P)]).then_inc(s_("vg_ready"), 1)
                wait_alone(pool, s_("v_out"), (L + 1) * DMA)
                wait_alone(pool, s_("sink_loaded"), (L + 1) * DMA)
                end_phase(pool)
                end_phase(pool)
                after_phase(pool, L, 8)
                with pool.Fori(0, 2) as j:
                    for par in range(2):
                        k = L * 4 + j * 2 + par
                        cs = bass.ds(j * (2 * N) + par * N, N)
                        wait_alone(pool, s_("xnew"), L * 4 + j * 2 + ONE)
                        for s in range(2):
                            gate = mod_dram[s, bass.ds(j * (2 * N) + 2 * D_MODEL + par * N, N)]
                            pool.dma_start(gb[par][:, s], gate.unsqueeze(0).to_broadcast([P, N])).then_inc(s_(f"gb_loaded{par}"), DMA)
                            pool.dma_start(xch[par][:, s], x_dram[s, :, cs]).then_inc(s_(f"gb_loaded{par}"), DMA)
                    for par in range(2):
                        cs = bass.ds(j * (2 * N) + par * N, N)
                        wait_alone(pool, s_("xnew"), L * 4 + j * 2 + par + 1 + ONE)
                        for s in range(2):
                            pool.dma_start(x_dram[s, :, cs], x2[:, s, cs]).then_inc(s_("x_stored"), DMA)
                    wait_alone(pool, s_("x_stored"), (L * 8 + j * 4 + 4) * DMA)
                end_phase(pool)

            after_phase(pool, DEPTH, 0)
            pool.dma_start(fng, a["final_norm_g"].unsqueeze(0).to_broadcast([P, D_MODEL])).then_inc(s_("fng_loaded"), DMA)
            rms(DEPTH + 1, D_MODEL, "ss_ready", "rstd_ready")
            wait_alone(pool, s_("y_final"), 1)
            for s, v in enumerate((o["y_prompt"][0], o["y_sample"][0])):
                pool.dma_start(v, x2[:, s]).then_inc(s_("y_out"), DMA)
            wait_alone(pool, s_("y_out"), 2 * DMA)


_INS = ["x_prompt", "x_sample", "c", "cache_k", "cache_v", "state_ssm_fwd", "state_ssm_bwd", "c_ctx", "norm_g", "w_mod",
        "b_mod", "w_in", "conv_w", "conv_b", "attn_sink", "a_log_fwd", "a_log_bwd", "dt_bias_fwd", "dt_bias_bwd", "d_skip",
        "ssd_norm_g", "w_pa", "w_ps", "w_out", "final_norm_g"]
_OUTS = [("y_prompt", (1, TOK, D_MODEL)), ("y_sample", (1, TOK, D_MODEL)),
         ("k_out", (1, DEPTH, TOK, N_KV, HEAD_DIM)), ("v_out", (1, DEPTH, TOK, N_KV, HEAD_DIM)),
         ("state_f_out", (1, DEPTH, NH, HP, D_STATE)), ("state_b_out", (1, DEPTH, NH, HP, D_STATE))]


def kernel(**inputs):
    import numpy as np
    import concourse.bacc as bacc
    from concourse.bass_utils import run_bass_kernel_spmd

    nc = bacc.Bacc("TRN2", target_bir_lowering=False, num_devices=1, dynamic_dma_scratch_size=8192)
    arrays, a = {}, {}
    inputs = dict(inputs, cst=constants())
    for name in _INS + ["cst"]:
        v = np.ascontiguousarray(inputs[name])
        arrays[f"in_{name}"] = v
        a[name] = nc.dram_tensor(f"in_{name}", v.shape, F32, kind="ExternalInput").ap()
    o = {n: nc.dram_tensor(f"out_{n}", s, F32, kind="ExternalOutput").ap() for n, s in _OUTS}
    build(nc, a, o)
    r = run_bass_kernel_spmd(nc, [arrays], core_ids=[0])
    return tuple(r.results[0][f"out_{n}"] for n, _ in _OUTS)
```

```python
from contextlib import ExitStack

import concourse.bass as bass
from concourse import mybir

F32 = mybir.dt.float32
F32R = mybir.dt.float32r
BF16 = mybir.dt.bfloat16
ACT = mybir.ActivationFunctionType
ALU = mybir.AluOpType
AX_X = mybir.AxisListType.X

P = 128
D_MODEL = 2048
DEPTH = 2
TOK = 128
HEAD_DIM = 128
N_Q = 16
N_KV = 4
KV_WIDTH = N_KV * HEAD_DIM
SSD_WIDTH = 2 * D_MODEL
HP = 64
NH = SSD_WIDTH // HP
NG = 8
HG = NH // NG
D_STATE = 128
BC_WIDTH = NG * D_STATE
D_CONV = 5
EPS = 1e-6
SCALE = HEAD_DIM ** -0.5
N = 512
KT = D_MODEL // P
IN_SPLITS = (D_MODEL, KV_WIDTH, KV_WIDTH, D_MODEL, SSD_WIDTH + 2 * BC_WIDTH, SSD_WIDTH, 2 * NH, D_MODEL, D_MODEL)
C_Q, C_K, C_V, C_ZA, C_XBC, C_ZS, C_DT, C_GA, C_GS = [sum(IN_SPLITS[:i]) for i in range(9)]
C_BC = C_XBC + SSD_WIDTH
IN_WIDTH = sum(IN_SPLITS)

NMOD = 3 * D_MODEL // N
MOD_FIRST = 8
MOD_GATE = NMOD - MOD_FIRST
PH_GATE = 0
PH_DT = PH_GATE + MOD_GATE
PH_BC = PH_DT + 1
PH_SSD = PH_BC + 4
PH_PS = PH_SSD + 2 * NG
PH_KV = PH_PS + 4 * 3
PH_Q = PH_KV + 2
PH_PA = PH_Q + 8


def ph_out(more):
    return PH_PA + (12 if more else 8)


CHUNKS = ph_out(True) + 8
U_BC = 0
U_SSD = U_BC + 2
U_PS = U_SSD + NG
U_KV = U_PS + 4
U_Q = U_KV + 1
U_PA = U_Q + 4
U_OUT = U_PA + 4
USES = U_OUT + 2
PHASES = 9
NQ = 17

K_ID, K_U, K_L, K_COS, K_SIN, K_NEG, K_SEL, K_COMB, K_WIDTH = 0, 128, 256, 384, 512, 640, 896, 904, 906


def constants():
    import numpy as np

    k = np.zeros((P, K_WIDTH), np.float32)
    t = np.arange(P)
    k[:, K_ID:K_ID + P] = np.eye(P)
    k[:, K_U:K_U + P] = t[:, None] <= t[None, :]
    k[:, K_L:K_L + P] = t[:, None] >= t[None, :]
    half = HEAD_DIM // 4
    freqs = (np.float32(10000.0) ** (-np.arange(half, dtype=np.float32) / np.float32(half))).astype(np.float32)
    for sec, pos in enumerate((t // 64, t % 64)):
        ang = pos.astype(np.float32)[:, None] * freqs[None, :]
        for hf, sign in enumerate((-1.0, 1.0)):
            at = sec * 64 + hf * 32
            k[:, K_COS + at:K_COS + at + 32] = np.cos(ang)
            k[:, K_SIN + at:K_SIN + at + 32] = sign * np.sin(ang)
    k[:, K_NEG:K_NEG + P] = np.where(t[:, None] > t[None, :], -1e30, 0.0)
    k[:, K_NEG + P:K_NEG + 2 * P] = np.where(t[:, None] < t[None, :], -1e30, 0.0)
    for h in range(HG):
        k[h, K_SEL + h] = 1.0
        k[64 + h, K_SEL + h] = 1.0
    for r in range(4):
        k[r, K_COMB + r % 2] = 1.0
    k[4, K_COMB:K_COMB + 2] = 1.0
    return k


class Chain:

    def __init__(self, eng, sem):
        self.eng, self.sem, self.n = eng, sem, 0

    def link(self, ins):
        ins.then_inc(self.sem, 1)
        self.n += 1
        return self.n

    def wait(self, n=None):
        self.eng.wait_ge(self.sem, self.n if n is None else n)

    def reset(self):
        if self.n:
            self.eng.wait_ge(self.sem, self.n)
            self.eng.sem_clear(self.sem)
            self.n = 0


def build(nc, a, o):
    with ExitStack() as ctx:
        def sb(name, shape, dt=F32):
            return ctx.enter_context(nc.sbuf_tensor(name, shape, dt))

        def sem(name):
            return ctx.enter_context(nc.semaphore(name))

        x_dram = nc.dram_tensor("x_scratch", (2, TOK, D_MODEL), F32).ap()
        mod_dram = nc.dram_tensor("mod_scratch", (2, 3 * D_MODEL), F32).ap()

        hT_h = sb("hT_h", [P, KT, 256], F32R)
        hT_l = sb("hT_l", [P, KT, 256], F32R)
        Z = sb("Z", [P, 2, 32, 256], F32R)
        yT_h, yT_l = Z[:, 0], Z[:, 1]
        aT_h, aT_l = Z[:, 0, 0:16], Z[:, 0, 16:32]
        mT_h, mT_l = Z[:, 1, 0:16], Z[:, 1, 16:32]
        raw = sb("raw", [P, 4, 2, N])
        w_h = sb("w_h", [P, 4, 2, N], F32R)
        w_l = sb("w_l", [P, 4, 2, N], F32R)
        X = sb("X", [P, 4096])
        x2 = X[:].rearrange("p (s n) -> p s n", s=2)
        xc = X[:, 0:1024]
        xt = X[:, 1024:2048].rearrange("p (s n) -> p s n", s=2)
        y = X[:, 2048:3072].rearrange("p (s n) -> p s n", s=2)
        zs = X[:, 3072:4096].rearrange("p (s n) -> p s n", s=2)
        arena = sb("arena", [P, 9728])
        used_to = [0]

        def part(n, at=None):
            at = used_to[0] if at is None else at
            used_to[0] = at + n
            assert used_to[0] <= 9728
            return arena[:, at:at + n]

        BC = part(4096, 0).rearrange("p (t n) -> p t n", n=256)
        BCg = part(512).rearrange("p (t n) -> p t n", n=256)
        Bt = part(128)
        CB = part(256).rearrange("p (s n) -> p s n", s=2)
        E = [part(512).rearrange("p (d s n) -> p d s n", d=2, s=2) for _ in range(2)]
        xw = part(1024).rearrange("p (d n) -> p d n", d=2)
        ST = part(1024).rearrange("p (d n) -> p d n", d=2)
        stload = part(1024).rearrange("p (d t n) -> p d t n", d=2, t=4)
        yoff = stload[:, 0].rearrange("p t n -> p (t n)")
        h32 = [part(1024, 0), part(1024)]
        rows = part(384).rearrange("p (t n) -> p t n", t=3)
        sq_dump = part(2048)
        modrow, modfin = part(512, 5120), part(512)
        dtz, dte, dtu, dtd, dtv = [part(256) for _ in range(5)]
        kT = part(1536, 0).rearrange("p (g b n) -> p g b n", g=4, b=3)
        vA = part(1536).rearrange("p (b n) -> p b n", b=3)
        qt = part(1024).rearrange("p (s n) -> p s n", s=2)
        qT = part(1024).rearrange("p (s h n) -> p s h n", s=2, h=4)
        Pc = part(512).rearrange("p (h n) -> p h n", h=4)
        Pl = part(1024).rearrange("p (h n) -> p h n", h=4)
        kraw = Pc.rearrange("p h n -> p (h n)")
        PT = part(1536).rearrange("p (b n) -> p b n", b=3)
        rtmp = PT[:, 0]
        zaT = part(1024)
        vg = part(384).rearrange("p (b n) -> p b n", b=3)
        sg = part(1024, 8704).rearrange("p (s n) -> p s n", s=2)
        m32 = part(1024, 0).rearrange("p (s n) -> p s n", s=2)
        gb = [part(1024, 1024 + 1024 * i).rearrange("p (s n) -> p s n", s=2) for i in range(2)]
        xch = [part(1024, 3072 + 1024 * i).rearrange("p (s n) -> p s n", s=2) for i in range(2)]
        fng = part(2048, 0)

        cst = sb("cst", [P, K_WIDTH])
        ident, Umat, Lmat = cst[:, K_ID:K_ID + P], cst[:, K_U:K_U + P], cst[:, K_L:K_L + P]
        one = cst[0:P, K_U + P - 1:K_U + P]
        neg = sb("neg", [P, 2, P], BF16)
        identb = sb("identb", [P, P], BF16)
        sel = sb("sel", [P, HG], F32R)
        cvec = sb("cvec", [P, 2, KT])
        csil = sb("csil", [P, 2, KT])
        cond = sb("cond", [P, KT, 4], F32R)
        chw = sb("chw", [P, 320])
        ng = sb("ng", [P, KT])
        arow = sb("arow", [P, 2 * NH])
        dtb = sb("dtb", [P, 2 * NH])
        sink = sb("sink", [P, N_Q])
        mcol = sb("mcol", [P, 2, 2, KT])
        SA = sb("SA", [P, NQ, NH])
        gs = sb("gs", [P, NQ, HG])
        dAg = sb("dAg", [P, 4, P])
        cw = [sb(f"cw{i}", [P, 6, 4]) for i in range(2)]
        nrm = [sb(f"nrm{i}", [P, 4]) for i in range(2)]
        H = sb("H", [P, 2, 2, P], F32R)
        half_exp = sb("half_exp", [P, 2])
        ss = sb("ss", [P, 2])
        rstd = sb("rstd", [P, 2])
        sm = sb("sm", [P, 6, 8])

        PM = ctx.enter_context(nc.psum_tensor("PM", [P, 4, 512], F32))
        A = ctx.enter_context(nc.psum_tensor("A", [P, 4, 512], F32))

        raw_loaded = [sem(f"raw_loaded{i}") for i in range(4)]
        hi_ready = sem("hi_ready")
        lo_ready = sem("lo_ready")
        w_used = sem("w_used")
        bank_free = [sem("bank_free0"), sem("bank_free1")]
        phase_done = {e: sem(f"phase_done_{e}") for e in ("pe", "act", "dve", "pool")}
        wait_passed = sem("wait_passed")
        act_chain, dve_chain, pool_chain = sem("act_chain"), sem("dve_chain"), sem("pool_chain")
        S = {}

        def s_(name):
            if name not in S:
                S[name] = sem(name)
            return S[name]

        me = [None]
        DMA = 16
        CR = 4
        ONE = 1
        START_AT_ONE = {
            "pe": ("y_part", "mod_sum", "q_T", "scores_done", "p_T", "o_done", "m_T"),
            "act": ("modrow_ready", "modrow_ready", "st_stored", "PT_ready", "conv_silu", "xt_ready"),
            "dve": ("yT_read", "a_read", "mT_ready", "sg_used", "aT_ready", "conv_done", "xnew", "modfin_ready"),
            "pool": ("ST_free", "modfin_free"),
        }

        def start_at_one(eng):
            for name in START_AT_ONE[me[0]]:
                eng.sem_inc(s_(name), ONE)

        block = ctx.enter_context(nc.Block())

        def m_banks(q):
            return PM[:, 2:4, :] if isinstance(q, int) and q == 3 else A[:, 0:2, :]

        def load_half(sp, c, i, src):
            wait_alone(sp, lo_ready, 8 * c + i + 1)
            n = src.shape[-1]
            sp.dma_start(raw[:, i % 4, :, 0:n], src).then_inc(raw_loaded[i % 4], DMA)

        def hi_half(act, c, i, n=N):
            act.wait_ge(raw_loaded[i % 4], (2 * c + i // 4 + 1) * DMA)
            act.wait_ge(w_used, 8 * c + i + 1)
            act.activation(w_h[:, i % 4, :, 0:n], raw[:, i % 4, :, 0:n], ACT.Copy).then_inc(hi_ready, 1)

        def lo_half(dve, c, i, n=N):
            dve.wait_ge(hi_ready, 8 * c + i + 1)
            dve.tensor_tensor(w_l[:, i % 4, :, 0:n], raw[:, i % 4, :, 0:n],
                              w_h[:, i % 4, :, 0:n].bitcast(F32), ALU.subtract).then_inc(lo_ready, 1)

        def mm_half(pe, c, i, kind, par, hi=None, lo=None, tile=None, last=7, n=N, bank=None):
            tile = i if tile is None else tile
            pe.wait_ge(lo_ready, 8 * c + i + 1 + CR)
            mm = None
            for kk in range(2):
                kt = 2 * tile + kk
                st, en = kt == 0, kt == 2 * last + 1
                wh, wl = w_h[:, i % 4, kk, 0:n], w_l[:, i % 4, kk, 0:n]
                if kind == "tok":
                    for s in range(2):
                        out = PM[:, 2 * par + s, 0:n] if n == N else A[:, 0, s * n:(s + 1) * n]
                        tk = slice(s * TOK, (s + 1) * TOK)
                        bank_first = st and (n == N or s == 0)
                        pe.matmul(out, hi[:, kt, tk], wh, start=bank_first, stop=False, skip_group_check=True)
                        pe.matmul(out, hi[:, kt, tk], wl, start=False, stop=False, skip_group_check=True)
                        mm = pe.matmul(out, lo[:, kt, tk], wh, start=False, stop=en, skip_group_check=True)
                elif kind == "ch":
                    for t in range(4):
                        out = PM[:, 2 * par + t // 2, (t % 2) * 256:(t % 2 + 1) * 256]
                        cs = slice(t * P, (t + 1) * P)
                        pe.matmul(out, wh[:, cs], hi[:, kt], start=st and t % 2 == 0, stop=False, skip_group_check=True)
                        pe.matmul(out, wh[:, cs], lo[:, kt], start=False, stop=False, skip_group_check=True)
                        mm = pe.matmul(out, wl[:, cs], hi[:, kt], start=False, stop=en, skip_group_check=True)
                else:
                    pe.matmul(bank, cond[:, kt], wh, start=st, stop=False, skip_group_check=True)
                    mm = pe.matmul(bank, cond[:, kt], wl, start=False, stop=en, skip_group_check=True)
            mm.then_inc(w_used, 1)

        def mod_first(L):
            return MOD_FIRST + L * NMOD

        def mod_half(pe, c, i, tile, T, par, k, same_bank=False):
            if tile == 0:
                pe.wait_ge(s_("modrow_ready"), k + 1 + (1 if same_bank else 0))
            mm_half(pe, c, i, "mod", None, tile=tile, bank=T[0:4, 2 * par])

        def mod_evac(act, T, par, k, c, i):
            act.wait_ge(w_used, 8 * c + i + 1 + CR)
            act.wait_ge(s_("mod_sum"), k + ONE)
            act.activation(modrow[0:4, :], T[0:4, 2 * par], ACT.Copy).then_inc(s_("modrow_ready"), 1)

        def mod_combine(pe, T, par, k):
            pe.wait_ge(s_("modrow_ready"), k + 1 + 2)
            pe.wait_ge(s_("modbias_loaded"), (k + 1) * DMA)
            wait_alone(pe, s_("modfin_ready"), k + ONE)
            pe.matmul(T[0:2, 2 * par + 1], cst[0:5, K_COMB:K_COMB + 2], modrow[0:5, :], start=True, stop=True,
                      skip_group_check=True).then_inc(s_("mod_sum"), 1)

        def mod_fin(dve, T, par, k):
            dve.wait_ge(s_("mod_sum"), k + 1 + ONE)
            dve.wait_ge(s_("modfin_free"), k + ONE)
            dve.tensor_copy(modfin[0:2, :], T[0:2, 2 * par + 1]).then_inc(s_("modfin_ready"), 1)

        def mod_io(pool, k, L, col):
            cs = span(col, N)
            wait_alone(pool, s_("mod_sum"), k + ONE)
            pool.dma_start(modrow[4:5, :], a["b_mod"][L, cs].unsqueeze(0)).then_inc(s_("modbias_loaded"), DMA)
            wait_alone(pool, s_("modfin_ready"), k + 1 + ONE)
            pool.dma_start(mod_dram[:, cs], modfin[0:2, :]).then_inc(s_("mod_stored"), DMA)
            wait_alone(pool, s_("mod_stored"), (k + 1) * DMA)
            pool.sem_inc(s_("modfin_free"), 1)

        def bank_wait(pe, par, use):
            pe.wait_ge(bank_free[par], use + 1)

        def chunk_done(eng, c, n=8):
            eng.wait_ge(w_used, 8 * c + n + CR)

        def wait_alone(eng, semaphore, value):
            eng.wait_ge(semaphore, value)
            eng.sem_inc(wait_passed, 1)

        def end_phase(eng):
            eng.drain().then_inc(phase_done[me[0]], 1)

        def after_phase(eng, L, idx):
            for e, semaphore in phase_done.items():
                if e != me[0]:
                    wait_alone(eng, semaphore, L * PHASES + idx + 1)

        def span(start, n):
            return slice(start, start + n) if isinstance(start, int) else bass.ds(start, n)

        def psum_sub(par, t):
            return PM[:, 2 * par + t // 2, (t % 2) * 256:(t % 2 + 1) * 256].rearrange("p (s n) -> p s n", s=2)

        @block.sync
        def _(sp):
            def cols(w, L, c0, kt0=0, n=N, natural=False):
                v = w[L].rearrange("(k p) n -> p k n", p=P) if natural else w[L].rearrange("(p k) n -> p k n", p=P)
                return v[:, kt0:kt0 + 2, span(c0, n)]

            def chunk(L, c, w, c0, halves=8, n=N, natural=False):
                for i in range(halves):
                    load_half(sp, c, i, cols(w, L, c0, 2 * i, n, natural))

            def mixed(L, c, w, c0, more, mod_col):
                for i in range(8):
                    load_half(sp, c, (2 if more else 1) * i, cols(w, L, c0, 2 * i, N, True))
                    if more:
                        load_half(sp, c, 2 * i + 1, cols(a["w_mod"], L + 1, mod_col, 2 * i))

            with sp.Fori(0, MOD_FIRST) as j:
                chunk(0, j, a["w_mod"], j * N)

            def layer(L, more):
                base = MOD_FIRST + L * CHUNKS
                with sp.Fori(0, MOD_GATE) as j:
                    chunk(L, base + PH_GATE + j, a["w_mod"], j * N + 2 * D_MODEL)
                chunk(L, base + PH_DT, a["w_in"], C_DT, n=2 * NH)
                with sp.Fori(0, 4) as j:
                    chunk(L, base + PH_BC + j, a["w_in"], j * N + C_BC)
                with sp.Fori(0, NG) as g:
                    chunk(L, base + PH_SSD + g * 2, a["w_in"], g * N + C_XBC)
                    chunk(L, base + PH_SSD + g * 2 + 1, a["w_in"], g * N + C_ZS)
                with sp.Fori(0, 4) as j:
                    chunk(L, base + PH_PS + j * 3, a["w_in"], j * N + C_GS)
                    chunk(L, base + PH_PS + j * 3 + 1, a["w_ps"], j * N, halves=16, natural=True)
                chunk(L, base + PH_KV, a["w_in"], C_K)
                chunk(L, base + PH_KV + 1, a["w_in"], C_V)
                with sp.Fori(0, 4) as g:
                    chunk(L, base + PH_Q + g * 2, a["w_in"], g * N + C_Q)
                    chunk(L, base + PH_Q + g * 2 + 1, a["w_in"], g * N + C_ZA)
                with sp.Fori(0, 4) as j:
                    c = base + PH_PA + j * (3 if more else 2)
                    chunk(L, c, a["w_in"], j * N + C_GA)
                    mixed(L, c + 1, a["w_pa"], j * N, more, j * N)
                with sp.Fori(0, 2) as j:
                    c = base + ph_out(more) + j * (4 if more else 2)
                    for par in range(2):
                        mixed(L, c + par * (2 if more else 1), a["w_out"], j * (2 * N) + par * N, more, j * (2 * N) + (4 + par) * N)

            with sp.Fori(0, DEPTH - 1) as layer_index:
                layer(layer_index, True)
            layer(DEPTH - 1, False)

        @block.tensor
        def _(pe):
            me[0] = "pe"
            start_at_one(pe)
            pe.sem_inc(w_used, CR)

            def halves(c, kind, par, use, hi, lo, steps, first=0, n_halves=8, mod=None):
                bank_wait(pe, par, use)
                for i in range(n_halves):
                    if mod:
                        mm_half(pe, c, 2 * i, kind, par, hi, lo, tile=i, last=n_halves - 1)
                        mod_half(pe, c, 2 * i + 1, i, *mod)
                    else:
                        mm_half(pe, c, i, kind, par, hi, lo, last=n_halves - 1)
                    for step in steps.get(first + i, ()):
                        step()

            def transpose(out, in_):
                return pe.transpose(out, in_, ident[0:in_.shape[0], 0:in_.shape[0]])

            def fp32(out, lhsT, rhs, start, stop=True):
                return pe.matmul(out, lhsT, rhs, start=start, stop=stop, skip_group_check=True)

            pe.wait_ge(s_("cond_ready"), 1)
            pe.wait_ge(s_("const_loaded"), DMA)
            pe.wait_ge(s_("const_cast"), 1)
            end_phase(pe)

            pe.wait_ge(bank_free[0], 1)
            pe.wait_ge(bank_free[1], 1)

            def mod_chunk(c, k, par, steps):
                for i in range(8):
                    mod_half(pe, c, i, i, PM, par, k)
                    for step in steps.get(i, ()):
                        step()

            def last_combined(k, par):
                return {2: [lambda: mod_combine(pe, PM, 1 - par, k - 1)]}
            mod_chunk(0, 0, 0, {})
            with pe.Fori(0, MOD_FIRST // 2 - 1) as j:
                for k, par in ((j * 2 + 1, 1), (j * 2 + 2, 0)):
                    mod_chunk(k, k, par, last_combined(k, par))
            mod_chunk(MOD_FIRST - 1, MOD_FIRST - 1, 1, last_combined(MOD_FIRST - 1, 1))
            mod_combine(pe, PM, 1, MOD_FIRST - 1)

            def layer(L, more):
                base, ub = MOD_FIRST + L * CHUNKS, L * USES
                kb = mod_first(L)

                def rows_T():
                    after_phase(pe, L, 0)
                    pe.wait_ge(s_("rows_loaded"), L * (4 * DMA) + 4 * DMA)
                    transpose(A[:, 3, 0:120], rows[0:120, 0])
                    transpose(A[:, 3, 120:240], rows[0:120, 1])
                    transpose(A[:, 3, 240:320], rows[0:80, 2]).then_inc(s_("rows_T"), 1)

                def x_T(q):
                    if q == 0:
                        pe.wait_ge(s_("xn_ready"), L + 1)
                    if q == 1:
                        pe.wait_ge(s_("chw_ready"), L + 1)
                    if q >= 2:
                        pe.wait_ge(s_("h32_ready"), L * 4 + q - 1)
                    for t in range(4):
                        for s in range(2):
                            v = x2[:, s, :].rearrange("p (c k) -> p k c", k=KT)[:, 4 * q + t, :]
                            mm = transpose(A[:, 2 * (q % 2) + t // 2, (t % 2) * 256 + s * P:(t % 2) * 256 + (s + 1) * P], v)
                    mm.then_inc(s_("xn_T"), 1)
                bank_wait(pe, 0, ub + U_BC)
                bank_wait(pe, 1, ub + U_BC)
                st = {3: [rows_T]}
                for q in range(4):
                    st[7 + 4 * q] = [lambda q=q: x_T(q)]
                for j in range(MOD_GATE):
                    steps = {i: list(st.get(8 * j + i, ())) for i in range(8)}
                    if j:
                        steps[2] += last_combined(kb + j, j % 2)[2]
                    mod_chunk(base + PH_GATE + j, kb + j, j % 2, steps)
                for i in range(8):
                    if i == 3:
                        mod_combine(pe, PM, (MOD_GATE - 1) % 2, kb + MOD_GATE - 1)
                    if i % 2 == 0:
                        pe.wait_ge(s_("hT_ready"), L * 4 + i // 2 + 1)
                    if i == 0:
                        pe.wait_ge(s_("h32_ready"), L * 4 + 4)
                    mm_half(pe, base + PH_DT, i, "tok", 0, hT_h, hT_l, n=2 * NH)
                end_phase(pe)
                end_phase(pe)

                def log_decays():
                    pe.wait_ge(s_("dA_ready"), L + 1)
                    fp32(A[:, 1, 0:256].rearrange("p (d s n) -> p d s n", d=2, s=2)[:, 0], Umat, SA[:, 8:10, :], True)
                    fp32(A[:, 1, 0:256].rearrange("p (d s n) -> p d s n", d=2, s=2)[:, 1], Lmat, SA[:, 10:12, :], False)
                    fp32(A[:, 1, 256:384].rearrange("p (d n) -> p d n", d=2), one.to_broadcast([P, P]),
                         SA[:, 8:12:2, :], False).then_inc(s_("acs_ready"), 1)
                wait_alone(pe, s_("modfin_ready"), kb + MOD_GATE + ONE)
                for j, st in enumerate(({}, {0: [log_decays]})):
                    halves(base + PH_BC + j * 2, "ch", 0, ub + U_BC + j, hT_h, hT_l, st)
                    halves(base + PH_BC + j * 2 + 1, "ch", 1, ub + U_BC + j, hT_h, hT_l, {})
                end_phase(pe)

                def ssd_steps(q):
                    G = L * NG + q

                    def start():
                        pe.wait_ge(s_("group_copied"), G + 1)
                        pe.wait_ge(s_("st_stored"), G + ONE)
                        for s in range(2):
                            fp32(A[:, 2, s * P:(s + 1) * P], BCg[:, 0, s * P:(s + 1) * P], BCg[:, 1, s * P:(s + 1) * P], s == 0)
                        fp32(A[:, 2, 256:384], BCg[:, 0, 0:P], ident, False).then_inc(s_("cb_done"), 1)
                        for ds in range(4):
                            mm = fp32(A[:, 3, ds * P:(ds + 1) * P], dAg[:, ds], (Umat, Lmat)[ds // 2], ds == 0)
                        mm.then_inc(s_("acsT_done"), 1)

                    def states_T():
                        pe.wait_ge(s_("xt_ready"), G + 1 + ONE)
                        pe.wait_ge(s_("st_loaded"), (G + 1) * 2 * DMA)
                        for d in range(2):
                            for t in range(4):
                                mm = transpose(A[:, d, t * P:(t + 1) * P], stload[:, d, t])
                        mm.then_inc(s_("stT_done"), 1)

                    def decay(h):
                        if h == 0:
                            pe.wait_ge(s_("H_ready"), G + 1)
                            pe.wait_ge(s_("cb_ready"), G + 1)
                            pe.wait_ge(s_("bt_ready"), G + 1)
                        if h >= 2:
                            pe.wait_ge(s_("exp_done"), G * HG + h - 1)
                        b = A[:, 2 + h % 2, :]
                        pe.matmul(b, sel[:, h:h + 1].to_broadcast([P, P]), H[:].rearrange("p d s n -> p (d s n)"),
                                  start=True, stop=False, skip_group_check=True)
                        mm = None
                        for d in range(2):
                            mm = pe.matmul(b[:, d * 256:(d + 1) * 256].rearrange("p (s n) -> p s n", s=2), identb[:],
                                           neg[:, d:d + 1, :].to_broadcast([P, 2, P]), start=False, stop=True,
                                           skip_group_check=True)
                        mm.then_inc(s_("decay_done"), 1)

                    def y_diag(h):
                        if h == 0:
                            pe.wait_ge(s_("ST_ready"), G + 1)
                        pe.wait_ge(s_("M_ready"), G * HG + h + 1)
                        for s in range(2):
                            for d in range(2):
                                mm = fp32(A[:, s, h * HP:(h + 1) * HP], E[h % 2][:, d, s, :], xt[:, s, h * HP:(h + 1) * HP],
                                          h == 0 and d == 0, stop=(d == 1))
                        mm.then_inc(s_("y_part"), 1)

                    def y_start():
                        pe.wait_ge(s_("exp_done"), G * HG + HG)
                        for d in range(2):
                            mm = fp32(A[:, 2 + d, :], BCg[:, 1, P:256], ST[:, d, :], True)
                        mm.then_inc(s_("yoff_done"), 1)

                    def final_states():
                        pe.wait_ge(s_("yoff_read"), G + 1)
                        pe.wait_ge(s_("xw_ready"), G + 1)
                        for d in range(2):
                            for t in range(4):
                                mm = fp32(A[:, 2 + d, t * P:(t + 1) * P], xw[:, d, t * P:(t + 1) * P], Bt, t == 0)
                        mm.then_inc(s_("stf_done"), 1)

                    def y_T():
                        pe.wait_ge(s_("yn_ready"), G + 1)
                        for t in range(4):
                            for s in range(2):
                                mm = transpose(A[:, t // 2, (t % 2) * 256 + s * P:(t % 2) * 256 + (s + 1) * P],
                                               y[:, s, t * P:(t + 1) * P])
                        mm.then_inc(s_("yT_done"), 1)

                    st = {0: [start], 1: [states_T], 12: [y_start], 14: [final_states], 15: [y_T]}
                    for h in range(HG):
                        st.setdefault(max(2, 2 + h), []).append(lambda h=h: decay(h))
                        st.setdefault(4 + h, []).append(lambda h=h: y_diag(h))
                    return st

                def xt_T(g):
                    pe.wait_ge(s_("xc_ready"), L * NG + g + 1)
                    pe.wait_ge(s_("yT_read"), L * NG + g + ONE)
                    for s in range(2):
                        for t in range(4):
                            mm = transpose(A[:, s, t * P:(t + 1) * P], xc[:, t * 256 + s * P:t * 256 + (s + 1) * P])
                    mm.then_inc(s_("xt_T"), 1)

                def ssd_body(g, steps):
                    st = dict(steps)
                    st[15] = list(st.get(15, ())) + [lambda: xt_T(g)]
                    halves(base + PH_SSD + g * 2, "ch", 0, ub + U_SSD + g, hT_h, hT_l, st)
                    halves(base + PH_SSD + g * 2 + 1, "tok", 1, ub + U_SSD + g, hT_h, hT_l, st, first=8)

                ssd_body(0, {})
                with pe.Fori(1, NG) as g:
                    ssd_body(g, ssd_steps(g - 1))
                end_phase(pe)

                def y_ready(n):
                    pe.wait_ge(s_("yT_read"), L * NG + n + ONE)

                def ps_body(j, steps):
                    halves(base + PH_PS + j * 3, "tok", 0, ub + U_PS + j, hT_h, hT_l, steps)
                    halves(base + PH_PS + j * 3 + 1, "tok", 1, ub + U_PS + j, yT_h, yT_l, steps, first=8, n_halves=16)
                st = ssd_steps(NG - 1)
                st[7] = list(st[7]) + [lambda: y_ready(NG - 1)]
                st[21] = [lambda: y_ready(NG)]
                ps_body(0, st)
                with pe.Fori(1, 4) as j:
                    ps_body(j, {})
                end_phase(pe)

                def k_T():
                    pe.wait_ge(s_("k_ready"), L + 1)
                    pe.wait_ge(s_("kv_loaded"), (L + 1) * 2 * DMA)
                    for b, src in enumerate((kraw, qt[:, 1], qt[:, 0])):
                        for h in range(N_KV):
                            mm = transpose(A[:, b, h * P:(h + 1) * P], src[:, h * P:(h + 1) * P])
                    mm.then_inc(s_("k_T"), 1)
                halves(base + PH_KV, "tok", 0, ub + U_KV, hT_h, hT_l, {})
                halves(base + PH_KV + 1, "tok", 1, ub + U_KV, hT_h, hT_l, {7: [k_T]})
                end_phase(pe)

                def q_scores(g):
                    G = L * 4 + g
                    pe.wait_ge(s_("q_ready"), G + 1)
                    pe.wait_ge(s_("kT_ready"), L + 1)
                    pe.wait_ge(s_("PT_ready"), G + ONE)
                    for s in range(2):
                        for h in range(4):
                            mm = transpose(A[:, s, h * P:(h + 1) * P], qt[:, s, h * P:(h + 1) * P])
                    mm.then_inc(s_("q_T"), 1)

                def scores(g):
                    G = L * 4 + g
                    pe.wait_ge(s_("qT_ready"), G + 1)
                    pe.wait_ge(s_("a_read"), G + ONE)
                    kTg = kT[:, span(g, 1), :, :].rearrange("p g b n -> p (g b n)")
                    for h in range(4):
                        fp32(A[:, 2, h * P:(h + 1) * P], qT[:, 0, h], kTg[:, 256:384], h == 0)
                    for h in range(4):
                        mm = fp32(A[:, h // 2, (h % 2) * 256:(h % 2 + 1) * 256], qT[:, 1, h], kTg[:, 0:256], h % 2 == 0)
                    mm.then_inc(s_("scores_done"), 1)

                def attn_steps(q):
                    G = L * 4 + q

                    def p_T():
                        pe.wait_ge(s_("p_ready"), G + 1)
                        for h in range(4):
                            transpose(A[:, 0, h * P:(h + 1) * P], Pl[:, h, 0:P])
                            transpose(A[:, 1, h * P:(h + 1) * P], Pl[:, h, P:256])
                            mm = transpose(A[:, 2, h * P:(h + 1) * P], Pc[:, h])
                        mm.then_inc(s_("p_T"), 1)

                    def pv():
                        pe.wait_ge(s_("PT_ready"), G + 1 + ONE)
                        pe.wait_ge(s_("vg_ready"), G + 1)
                        fp32(A[:, 3, :], vg[:, 2], PT[:, 2], True)
                        fp32(A[:, 2, :], vg[:, 0], PT[:, 0], True, stop=False)
                        fp32(A[:, 2, :], vg[:, 1], PT[:, 1], False).then_inc(s_("o_done"), 1)
                    return {0: [lambda: scores(q)], 3: [p_T], 5: [pv]}

                def q_body(g, steps):
                    st = dict(steps)
                    st[13] = [lambda: q_scores(g)]
                    halves(base + PH_Q + g * 2, "tok", 0, ub + U_Q + g, hT_h, hT_l, st)
                    halves(base + PH_Q + g * 2 + 1, "ch", 1, ub + U_Q + g, hT_h, hT_l, st, first=8)
                q_body(0, {})
                with pe.Fori(1, 4) as g:
                    q_body(g, attn_steps(g - 1))
                end_phase(pe)

                def a_ready(n):
                    pe.wait_ge(s_("a_read"), L * 4 + 4 + ONE)
                    pe.wait_ge(s_("aT_ready"), L * 4 + n + ONE)

                def m_T(q):
                    pe.wait_ge(s_("m_ready"), L * 4 + q + 1)
                    pe.wait_ge(s_("mT_ready"), L * 4 + q + ONE)
                    for t in range(4):
                        for s in range(2):
                            mm = transpose(m_banks(q)[:, t // 2, (t % 2) * 256 + s * P:(t % 2) * 256 + (s + 1) * P],
                                           m32[:, s, t * P:(t + 1) * P])
                    mm.then_inc(s_("m_T"), 1)

                kn = kb + MOD_GATE

                def pa_body(j, steps):
                    c = base + PH_PA + j * (3 if more else 2)
                    halves(c, "tok", 0, ub + U_PA + j, hT_h, hT_l, steps)
                    halves(c + 1, "tok", 1, ub + U_PA + j, aT_h, aT_l, steps, first=8, mod=(A, 1, kn + j, True) if more else None)
                st = attn_steps(3)
                st[7] = [lambda: a_ready(3)]
                st[13] = [lambda: a_ready(4)]
                pa_body(0, st)
                with pe.Fori(1, 4) as j:
                    st = {5: [lambda: m_T(j - 1)]}
                    if more:
                        st[2] = [lambda: mod_combine(pe, A, 1, kn + j - 1)]
                    pa_body(j, st)
                end_phase(pe)

                def m_ready(n):
                    wait_alone(pe, s_("mT_ready"), L * 4 + n + ONE)
                m_ready(3)
                for j in range(2):
                    c = base + ph_out(more) + j * (4 if more else 2)
                    for par in range(2):
                        kk = kn + 4 + j * 2 + par
                        st = {1: [lambda: mod_combine(pe, A, 1 - par, kk - 1)]} if more else {}
                        if j == 0 and par == 0:
                            st[2] = [lambda: m_T(3)]
                            st[5] = [lambda: m_ready(4)]
                        halves(c + par * (2 if more else 1), "tok", par, ub + U_OUT + j, mT_h, mT_l, st,
                               mod=(A, par, kk) if more else None)
                if more:
                    mod_combine(pe, A, 1, kn + 7)
                end_phase(pe)

            with pe.Fori(0, DEPTH - 1) as layer_index:
                layer(layer_index, True)
            layer(DEPTH - 1, False)

        @block.scalar
        def _(act):
            me[0] = "act"
            start_at_one(act)
            ch = Chain(act, act_chain)
            F = ACT

            def halves(c, steps, first=0, n_halves=8, n=N, mod=False):
                for i in range(n_halves):
                    if mod:
                        hi_half(act, c, 2 * i)
                        hi_half(act, c, 2 * i + 1)
                    else:
                        hi_half(act, c, i, n)
                    for step in steps.get(first + i, ()):
                        step()

            act.wait_ge(s_("const_loaded"), DMA)
            act.activation(neg[:], cst[:, K_NEG:K_NEG + 2 * P].rearrange("p (d n) -> p d n", d=2), F.Copy)
            act.activation(identb[:], ident, F.Copy)
            act.activation(sel[:], cst[:, K_SEL:K_SEL + HG], F.Copy).then_inc(s_("const_cast"), 1)
            act.wait_ge(s_("cvec_loaded"), 2 * DMA)
            ch.link(act.activation(csil[:], cvec[:], F.Silu))
            ch.wait()
            act.activation(cond[:, :, 0:2].rearrange("p k s -> p s k"), csil[:], F.Copy).then_inc(s_("cond_hi"), 1)
            ch.reset()
            end_phase(act)

            def last_rows(k, par, c):
                return {3: [lambda: mod_evac(act, PM, 1 - par, k - 1, c - 1, 7)]}
            halves(0, {})
            with act.Fori(0, MOD_FIRST // 2 - 1) as j:
                for k, par in ((j * 2 + 1, 1), (j * 2 + 2, 0)):
                    halves(k, last_rows(k, par, k))
            halves(MOD_FIRST - 1, last_rows(MOD_FIRST - 1, 1, MOD_FIRST - 1))
            mod_evac(act, PM, 1, MOD_FIRST - 1, MOD_FIRST - 1, 7)

            def layer(L, more):
                base = MOD_FIRST + L * CHUNKS
                kb = mod_first(L)

                def squares_x():
                    after_phase(act, L, 0)
                    act.wait_ge(s_("x_ready"), L + 1)
                    for s in range(2):
                        if s:
                            ch.wait()
                        ch.link(act.activation(sq_dump, x2[:, s], F.Square, accum_out=ss[:, s:s + 1]))
                    ch.wait()
                    act.activation(sm[:, 0, 0:2], ss[:], F.Copy).then_inc(s_("ss_ready"), 1)
                    ch.reset()

                def params():
                    act.wait_ge(s_("rows_T"), L + 1)
                    act.activation(chw[:], A[:, 3, 0:320], F.Copy).then_inc(s_("chw_ready"), 1)
                    act.wait_ge(s_("small_loaded"), (L + 1) * 6 * DMA)
                    act.activation(arow[:], arow[:], F.Exp).then_inc(s_("arow_exp"), 1)

                def h_hi(q):
                    act.wait_ge(s_("h32_ready"), L * 4 + q + 1)
                    act.activation(hT_h[:, 4 * q:4 * q + 4].rearrange("p k n -> p (k n)"), h32[q % 2], F.Copy)\
                        .then_inc(s_("hT_hi"), 1)
                st = {0: [squares_x], 4: [params]}
                for q in range(4):
                    st[8 + 4 * q] = [lambda q=q: h_hi(q)]
                for j in range(MOD_GATE):
                    if j:
                        st.setdefault(8 * j + 3, []).extend(last_rows(kb + j, j % 2, base + PH_GATE + j)[3])
                    halves(base + PH_GATE + j, st, first=8 * j)
                halves(base + PH_DT, {3: [lambda: mod_evac(act, PM, (MOD_GATE - 1) % 2, kb + MOD_GATE - 1, base + PH_DT - 1, 7)]},
                       n=2 * NH)

                def dt_exp():
                    act.wait_ge(s_("dt_abs"), L + 1)
                    act.activation(dte, dtd, F.Exp, scale=-1.0).then_inc(s_("dt_exp"), 1)

                def dt_ln():
                    act.wait_ge(s_("dt_u"), L + 1)
                    act.activation(dtv, dtu, F.Ln).then_inc(s_("dt_ln"), 1)
                    end_phase(act)
                    end_phase(act)

                def center(k):
                    chunk_done(act, base + PH_BC + k)
                    act.wait_ge(s_("cw_copied"), L * 12 + k + 1)
                    act.wait_ge(s_("conv_silu"), L * 12 + k + ONE)
                    for t in range(4):
                        mm = act.activation(xc[:, t * 256:(t + 1) * 256].rearrange("p (s n) -> p s n", s=2),
                                            psum_sub(k % 2, t), F.Identity,
                                            bias=cw[k % 2][:, 5, t:t + 1], scale=cw[k % 2][:, 2, t:t + 1])
                    mm.then_inc(s_("conv_center"), 1)

                def bc_silu(k):
                    act.wait_ge(s_("conv_done"), L * 12 + k + 1 + ONE)
                    act.activation(BC[:, 4 * k:4 * k + 4, :].rearrange("p t n -> p (t n)"), xc, F.Silu)\
                        .then_inc(s_("conv_silu"), 1)

                def decays():
                    act.wait_ge(s_("tail_ready"), L + 1)
                    act.activation(SA[:, 14:16, :], SA[:, 1:4:2, :], F.Exp, scale=-1.0)
                    act.activation(SA[:, 12:14, :], SA[:, 12:14, :], F.Exp).then_inc(s_("ew_exp"), 1)

                for j, st in enumerate(({4: [dt_exp], 5: [dt_ln]},
                                        {3: [lambda: center(1)], 5: [lambda: bc_silu(1)], 6: [decays]})):
                    st[11] = [lambda: center(2 * j)]
                    st[13] = [lambda: bc_silu(2 * j)]
                    halves(base + PH_BC + j * 2, st)
                    halves(base + PH_BC + j * 2 + 1, st, first=8)

                def ssd_steps(q):
                    G = L * NG + q

                    def evacs():
                        act.wait_ge(s_("xt_T"), G + 1)
                        act.activation(xt[:], A[:, 0:2, :], F.Copy).then_inc(s_("xt_ready"), 1)
                        chunk_done(act, base + PH_SSD + q * 2 + 1)
                        act.activation(zs[:], PM[:, 2:4, :], F.Silu).then_inc(bank_free[1], 1)

                    def H_hi():
                        act.wait_ge(s_("acsT_done"), G + 1)
                        act.activation(H[:].rearrange("p d s n -> p (d s n)"), A[:, 3, :], F.Copy).then_inc(s_("H_hi"), 1)
                        act.wait_ge(s_("cb_ready"), G + 1)
                        act.activation(Bt, A[:, 2, 256:384], F.Copy).then_inc(s_("bt_ready"), 1)

                    def ST_copy():
                        act.wait_ge(s_("stT_done"), G + 1)
                        act.wait_ge(s_("ST_free"), G + ONE)
                        act.activation(ST[:], A[:, 0:2, :], F.Copy).then_inc(s_("ST_ready"), 1)

                    def exp(h):
                        act.wait_ge(s_("decay_done"), G * HG + h + 1)
                        if h >= 2:
                            act.wait_ge(s_("y_part"), G * HG + h - 1 + ONE)
                        for d in range(2):
                            for s in range(2):
                                mm = act.activation(E[h % 2][:, d, s, :], A[:, 2 + h % 2, (2 * d + s) * P:(2 * d + s + 1) * P],
                                                    F.Exp, bias=gs[:, 2 * d + s, h:h + 1])
                        mm.then_inc(s_("exp_done"), 1)

                    def stores():
                        act.wait_ge(s_("stf_done"), G + 1)
                        act.activation(ST[:], A[:, 2:4, :], F.Copy).then_inc(s_("st_stored"), 1)

                    def squares():
                        act.wait_ge(s_("yz_ready"), G + 1)
                        for s in range(2):
                            if s:
                                ch.wait()
                            ch.link(act.activation(E[0].rearrange("p d s n -> p (d s n)"), y[:, s], F.Square, accum_out=ss[:, s:s + 1]))
                        ch.wait()
                        act.activation(sm[:, 0, 0:2], ss[:], F.Copy).then_inc(s_("yss_ready"), 1)

                    def y_hi():
                        act.wait_ge(s_("yT_done"), G + 1)
                        act.wait_ge(s_("nrm_copied"), G + 1)
                        for t in range(4):
                            mm = act.activation(yT_h[:, span(q * 4 + t, 1), :],
                                                A[:, t // 2:t // 2 + 1, (t % 2) * 256:(t % 2 + 1) * 256], F.Copy,
                                                scale=nrm[0][:, t:t + 1])
                        mm.then_inc(s_("y_hi"), 1)
                    st = {2: [evacs], 3: [H_hi], 4: [ST_copy], 13: [], 14: [squares]}
                    for h in range(HG):
                        st.setdefault(4 + h, []).append(lambda h=h: exp(h))
                    st[15] = [stores, y_hi]
                    return st

                def conv(g):
                    chunk_done(act, base + PH_SSD + g * 2)
                    act.wait_ge(s_("cw_copied"), L * 12 + 4 + g + 1)
                    act.wait_ge(s_("conv_silu"), L * 12 + 4 + g + ONE)
                    act.wait_ge(s_("xt_ready"), L * NG + g + ONE)
                    for t in range(4):
                        mm = act.activation(xc[:, t * 256:(t + 1) * 256].rearrange("p (s n) -> p s n", s=2),
                                            psum_sub(0, t), F.Identity,
                                            bias=cw[0][:, 5, t:t + 1], scale=cw[0][:, 2, t:t + 1])
                    mm.then_inc(s_("conv_center"), 1)

                def silu(g):
                    act.wait_ge(s_("conv_done"), L * 12 + 4 + g + 1 + ONE)
                    ins = act.activation(xc, xc, F.Silu)
                    ins.then_inc(s_("xc_ready"), 1)
                    act.wait_ge(s_("xc_ready"), L * NG + g + 1)
                    act.sem_inc(s_("conv_silu"), 1)

                def ssd_body(g, steps):
                    st = {k: list(v) for k, v in steps.items()}
                    st[11] = [lambda: conv(g)] + st.get(11, [])
                    st[15] = [lambda: silu(g)] + st.get(15, [])
                    halves(base + PH_SSD + g * 2, st)
                    halves(base + PH_SSD + g * 2 + 1, st, first=8)
                    ch.reset()
                ssd_body(0, {3: [lambda: center(3)], 5: [lambda: bc_silu(3), lambda: end_phase(act)]})
                with act.Fori(1, NG) as g:
                    ssd_body(g, ssd_steps(g - 1))
                end_phase(act)

                def sigmoid(c, use):
                    chunk_done(act, c)
                    act.wait_ge(s_("sg_used"), L * 8 + use + ONE)
                    act.activation(sg[:], PM[:, 0:2, :], F.Sigmoid).then_inc(s_("sg_ready"), 1)
                    act.wait_ge(s_("sg_ready"), L * 8 + use + 1)
                    act.sem_inc(bank_free[0], 1)
                def ps_body(j, steps):
                    st = {k: list(v) for k, v in steps.items()}
                    st[11] = [lambda: sigmoid(base + PH_PS + j * 3, j)] + st.get(11, [])
                    halves(base + PH_PS + j * 3, st)
                    halves(base + PH_PS + j * 3 + 1, st, first=8, n_halves=16)
                ps_body(0, ssd_steps(NG - 1))
                ch.reset()
                with act.Fori(1, 4) as j:
                    ps_body(j, {})
                end_phase(act)

                def k_evac():
                    after_phase(act, L, 5)
                    chunk_done(act, base + PH_KV)
                    act.activation(qt[:, 0], PM[:, 0], F.Copy).then_inc(s_("kc_ready"), 1)

                def kT_evac():
                    act.wait_ge(s_("k_T"), L + 1)
                    act.activation(kT[:].rearrange("p g b n -> p b g n"),
                                   A[:, 0:3, :].rearrange("p b (g n) -> p b g n", g=4), F.Copy).then_inc(s_("kT_ready"), 1)
                    chunk_done(act, base + PH_KV + 1)
                    act.wait_ge(s_("kv_loaded"), (L + 1) * 2 * DMA)
                    act.activation(vA[:, 2], PM[:, 2], F.Copy)
                    act.activation(vA[:, 1], PM[:, 3], F.Copy).then_inc(bank_free[1], 1)
                halves(base + PH_KV, {})
                halves(base + PH_KV + 1, {3: [k_evac]})

                def kv_left():
                    kT_evac()
                    end_phase(act)

                def q_evac(g):
                    chunk_done(act, base + PH_Q + g * 2)
                    act.wait_ge(s_("q_T"), L * 4 + g + ONE)
                    act.activation(qt[:, 0], PM[:, 0], F.Copy).then_inc(s_("qc_ready"), 1)

                def qT_evac(g):
                    act.wait_ge(s_("q_T"), L * 4 + g + 1 + ONE)
                    act.wait_ge(s_("scores_done"), L * 4 + g + ONE)
                    act.activation(qT[:].rearrange("p s h n -> p s (h n)"), A[:, 0:2, :], F.Copy).then_inc(s_("qT_ready"), 1)

                def soft(g):
                    act.wait_ge(s_("nm_ready"), L * 4 + g + 1)
                    act.wait_ge(s_("p_T"), L * 4 + g + ONE)
                    for h in range(4):
                        act.activation(Pc[:, h], A[:, 2, h * P:(h + 1) * P], F.Exp, bias=sm[:, 1, h:h + 1], scale=SCALE,
                                       accum_out=sm[:, 2, h:h + 1])
                    for h in range(4):
                        act.activation(Pl[:, h], A[:, h // 2, (h % 2) * 256:(h % 2 + 1) * 256], F.Exp,
                                       bias=sm[:, 1, 4 + h:5 + h], scale=SCALE, accum_out=sm[:, 2, 4 + h:5 + h])
                    act.activation(sm[:, 4], sm[:, 3], F.Exp).then_inc(s_("exps_done"), 1)

                def attn_steps(q):
                    G = L * 4 + q

                    def pT_evac():
                        act.wait_ge(s_("p_T"), G + 1 + ONE)
                        act.activation(PT[:], A[:, 0:3, :], F.Copy).then_inc(s_("PT_ready"), 1)
                        chunk_done(act, base + PH_Q + q * 2 + 1)
                        act.wait_ge(s_("aT_ready"), G + ONE)
                        act.activation(zaT, PM[:, 2:4, :].rearrange("p b n -> p (b n)"), F.Silu).then_inc(bank_free[1], 1)

                    def a_hi():
                        act.wait_ge(s_("a_read"), G + 1 + ONE)
                        act.activation(aT_h[:, span(q * 4, 4), :],
                                       zaT.rearrange("p (k n) -> p k n", k=4), F.Copy).then_inc(s_("a_hi"), 1)
                    return {1: [lambda: qT_evac(q)], 4: [lambda: soft(q)], 7: [pT_evac], 8: [a_hi]}

                def q_body(g, steps):
                    st = {k: list(v) for k, v in steps.items()}
                    st[11] = [lambda: q_evac(g)]
                    halves(base + PH_Q + g * 2, st)
                    halves(base + PH_Q + g * 2 + 1, st, first=8)
                q_body(0, {3: [kv_left], 10: [lambda: after_phase(act, L, 6)]})
                with act.Fori(1, 4) as g:
                    q_body(g, attn_steps(g - 1))
                end_phase(act)

                def m_hi(q):
                    act.wait_ge(s_("m_T"), L * 4 + q + 1 + ONE)
                    act.activation(mT_h[:, span(q * 4, 4), :],
                                   m_banks(q).rearrange("p b (k n) -> p (b k) n", k=2), F.Copy).then_inc(s_("m_hi"), 1)

                kn = kb + MOD_GATE

                def pa_body(j, steps):
                    c = base + PH_PA + j * (3 if more else 2)
                    st = {k: list(v) for k, v in steps.items()}
                    st[11] = [lambda: sigmoid(c, j + 4)]
                    halves(c, st)
                    halves(c + 1, st, first=8, mod=more)

                def attention_left():
                    act.wait_ge(s_("aT_ready"), L * 4 + 4 + ONE)
                st = attn_steps(3)
                st[10] = [attention_left]
                pa_body(0, st)
                with act.Fori(1, 4) as j:
                    st = {6: [lambda: m_hi(j - 1)]}
                    if more:
                        st[3] = [lambda: mod_evac(act, A, 1, kn + j - 1, base + PH_PA + j * 3 - 2, 15)]
                    pa_body(j, st)
                for j in range(2):
                    c = base + ph_out(more) + j * (4 if more else 2)
                    for par in range(2):
                        cc, kk = c + par * (2 if more else 1), kn + 4 + j * 2 + par
                        st = {3: [lambda: mod_evac(act, A, 1 - par, kk - 1, cc - 2, 15)]} if more else {}
                        if j == 0 and par == 0:
                            st[5] = [lambda: m_hi(3), lambda: end_phase(act)]
                        halves(cc, st, mod=more)
                if more:
                    mod_evac(act, A, 1, kn + 7, base + ph_out(more) + 6, 15)
                end_phase(act)

            with act.Fori(0, DEPTH - 1) as layer_index:
                layer(layer_index, True)
            layer(DEPTH - 1, False)

            after_phase(act, DEPTH, 0)
            for s in range(2):
                if s:
                    ch.wait()
                ch.link(act.activation(arena[:, 2048:4096], x2[:, s], F.Square, accum_out=ss[:, s:s + 1]))
            ch.wait()
            act.activation(sm[:, 0, 0:2], ss[:], F.Copy).then_inc(s_("ss_ready"), 1)

        @block.vector
        def _(dve):
            me[0] = "dve"
            start_at_one(dve)
            dve.sem_inc(lo_ready, CR)
            ch = Chain(dve, dve_chain)

            def halves(c, steps, first=0, n_halves=8, n=N, mod=False):
                for i in range(n_halves):
                    if mod:
                        lo_half(dve, c, 2 * i)
                        lo_half(dve, c, 2 * i + 1)
                    else:
                        lo_half(dve, c, i, n)
                    for step in steps.get(first + i, ()):
                        step()

            def tt(out, a_, b_, op):
                return dve.tensor_tensor(out, a_, b_, op)

            dve.sem_inc(bank_free[0], 1)
            dve.sem_inc(bank_free[1], 1)
            dve.memset(half_exp[:], -0.5).then_inc(s_("half_exp_set"), 1)
            dve.wait_ge(s_("cond_hi"), 1)
            tt(cond[:, :, 2:4].rearrange("p k s -> p s k"), csil[:],
               cond[:, :, 0:2].bitcast(F32).rearrange("p k s -> p s k"), ALU.subtract).then_inc(s_("cond_ready"), 1)
            end_phase(dve)

            def rope(src, out):
                x = src.rearrange("p (h c f w) -> p h c f w", h=4, c=2, f=2)
                cos = cst[:, K_COS:K_COS + P].rearrange("p (c f w) -> p c f w", c=2, f=2)
                sin = cst[:, K_SIN:K_SIN + P].rearrange("p (c f w) -> p c f w", c=2, f=2)
                r = rtmp.rearrange("p (h c f w) -> p h c f w", h=4, c=2, f=2)
                ov = out.rearrange("p (h n) -> p h n", h=4)
                tt(ov, src.rearrange("p (h n) -> p h n", h=4),
                   cst[:, K_COS:K_COS + P].unsqueeze(1).to_broadcast([P, 4, P]), ALU.mult)
                for f in range(2):
                    for c in range(2):
                        k = tt(r[:, :, c, f], x[:, :, c, 1 - f],
                               sin[:, c, f].unsqueeze(1).to_broadcast([P, 4, 32]), ALU.mult)
                ch.link(k)
                ch.wait()
                return tt(out, out, rtmp, ALU.add)

            tap_done = {}

            def conv_taps(par, cbuf, taps=(0, 1, 3, 4)):
                at = []
                for t in range(4):
                    acc = xc[:, t * 256:(t + 1) * 256].rearrange("p (s n) -> p s n", s=2)
                    at.append((acc, psum_sub(par, t)))
                for j in taps:
                    d = j - 2
                    lo_, hi_ = max(0, -d), TOK - max(0, d)
                    for t, (acc, u) in enumerate(at):
                        if j > 0:
                            ch.wait(tap_done[t])
                        o_ = acc[:, :, lo_:hi_]
                        ins = dve.scalar_tensor_tensor(out=o_, in0=u[:, :, lo_ + d:hi_ + d], scalar=cw[cbuf][:, j, t:t + 1],
                                                       in1=o_, op0=ALU.mult, op1=ALU.add)
                        if not (j == 4 and t == 3):
                            tap_done[t] = ch.link(ins)
                if taps[-1] == 4:
                    ins.then_inc(bank_free[par], 1)

            def last_sum(k, par):
                return {5: [lambda: mod_fin(dve, PM, 1 - par, k - 1)]}
            halves(0, {})
            with dve.Fori(0, MOD_FIRST // 2 - 1) as j:
                for k, par in ((j * 2 + 1, 1), (j * 2 + 2, 0)):
                    halves(k, last_sum(k, par))
            halves(MOD_FIRST - 1, last_sum(MOD_FIRST - 1, 1))
            mod_fin(dve, PM, 1, MOD_FIRST - 1)

            def layer(L, more):
                base, ub = MOD_FIRST + L * CHUNKS, L * USES
                kb = mod_first(L)

                def norm_x():
                    after_phase(dve, L, 0)
                    dve.wait_ge(s_("rstd_ready"), L + 1)
                    for s in range(2):
                        ins = dve.tensor_scalar(x2[:, s], x2[:, s], rstd[:, s:s + 1], None, ALU.mult)
                    ins.then_inc(s_("xn_ready"), 1)

                def params():
                    dve.wait_ge(s_("arow_exp"), L + 1)
                    dve.tensor_scalar(arow[:], arow[:], -1.0, None, ALU.mult).then_inc(s_("arow_ready"), 1)
                    dve.wait_ge(s_("mcol_loaded"), (L + 1) * 4 * DMA)
                    dve.wait_ge(s_("small_loaded"), (L + 1) * 6 * DMA)
                    ch.link(dve.scalar_tensor_tensor(out=mcol[:, :, 1, :], in0=mcol[:, :, 1, :], scalar=1.0,
                                                     in1=ng[:].unsqueeze(1).to_broadcast([P, 2, KT]), op0=ALU.add, op1=ALU.mult))
                    ch.wait()

                def h(q):
                    dve.wait_ge(s_("xn_T"), L * 4 + q + 1)
                    if q >= 2:
                        dve.wait_ge(s_("hT_ready"), L * 4 + q - 1)
                    for t in range(4):
                        for s in range(2):
                            at = t * 256 + s * P
                            kt = 4 * q + t
                            ins = dve.tensor_scalar(h32[q % 2][:, at:at + P],
                                                    A[:, 2 * (q % 2) + t // 2, at % 512:at % 512 + P],
                                                    mcol[:, s, 1, kt:kt + 1], mcol[:, s, 0, kt:kt + 1], ALU.mult, ALU.add)
                    ins.then_inc(s_("h32_ready"), 1)
                    dve.wait_ge(s_("hT_hi"), L * 4 + q + 1)
                    hs = hT_h[:, 4 * q:4 * q + 4].rearrange("p k n -> p (k n)")
                    tt(hT_l[:, 4 * q:4 * q + 4].rearrange("p k n -> p (k n)"), h32[q % 2], hs.bitcast(F32), ALU.subtract)\
                        .then_inc(s_("hT_ready"), 1)
                st = {3: [norm_x], 5: [params]}
                for q in range(4):
                    st[8 + 4 * q] = [lambda q=q: h(q)]
                for j in range(MOD_GATE):
                    if j:
                        st.setdefault(8 * j + 5, []).extend(last_sum(kb + j, j % 2)[5])
                    halves(base + PH_GATE + j, st, first=8 * j)
                halves(base + PH_DT, {5: [lambda: mod_fin(dve, PM, (MOD_GATE - 1) % 2, kb + MOD_GATE - 1)]}, n=2 * NH)

                def dt_abs():
                    chunk_done(dve, base + PH_DT)
                    z4 = dtz.rearrange("p (s n) -> p s n", s=2)
                    ch.link(tt(z4, A[:, 0, 0:256].rearrange("p (s n) -> p s n", s=2),
                               dtb[:].unsqueeze(1).to_broadcast([P, 2, 2 * NH]), ALU.add))
                    ch.wait()
                    dve.scalar_tensor_tensor(out=dtd, in0=dtz, scalar=-1.0, in1=dtz, op0=ALU.mult, op1=ALU.max).then_inc(s_("dt_abs"), 1)

                def dt_u():
                    dve.wait_ge(s_("dt_exp"), L + 1)
                    dve.tensor_scalar(dtu, dte, 1.0, None, ALU.add).then_inc(s_("dt_u"), 1)

                def dt_end():
                    dve.wait_ge(s_("dt_u"), L + 1)
                    ch.link(dve.tensor_scalar(dtd, dtu, -1.0, None, ALU.add))
                    ch.wait()
                    ch.link(tt(dte, dte, dtd, ALU.subtract))
                    dve.wait_ge(s_("dt_ln"), L + 1)
                    ch.link(dve.reciprocal(dtu, dtu))
                    ch.wait()
                    ch.link(tt(dte, dte, dtu, ALU.mult))
                    ch.link(dve.scalar_tensor_tensor(out=dtz, in0=dtz, scalar=0.0, in1=dtv, op0=ALU.max, op1=ALU.add))
                    ch.wait()
                    dt_v = SA[:, 4:8, :].rearrange("p (d s) n -> p s d n", d=2)
                    ch.link(tt(dt_v, dte.rearrange("p (s d n) -> p s d n", s=2, d=2),
                               dtz.rearrange("p (s d n) -> p s d n", s=2, d=2), ALU.add))
                    ch.wait()
                    for d in range(2):
                        ins = tt(SA[:, 8 + 2 * d:10 + 2 * d, :], SA[:, 4 + 2 * d:6 + 2 * d, :],
                                 arow[:, d * NH:(d + 1) * NH].unsqueeze(1).to_broadcast([P, 2, NH]), ALU.mult)
                    ins.then_inc(s_("dA_ready"), 1)
                    end_phase(dve)
                    end_phase(dve)

                def conv_bc(k):
                    dve.wait_ge(s_("conv_center"), L * 12 + k + 1)
                    conv_taps(k % 2, k % 2)
                    dve.wait_ge(bank_free[k % 2], ub + U_BC + k // 2 + 2)
                    dve.sem_inc(s_("conv_done"), 1)

                def cumulative():
                    dve.wait_ge(s_("acs_ready"), L + 1)
                    ch.link(dve.tensor_scalar(SA[:, 0:4, :].rearrange("p q n -> p (q n)"), A[:, 1, 0:256], -1.0, None, ALU.mult))
                    ch.wait()
                    tt(SA[:, 12:14, :], A[:, 1, 256:384].rearrange("p (d n) -> p d n", d=2), SA[:, 0:4:2, :], ALU.add)\
                        .then_inc(s_("tail_ready"), 1)

                def decay_dt():
                    dve.wait_ge(s_("ew_exp"), L + 1)
                    ch.link(tt(SA[:, 12:14, :], SA[:, 12:14, :], SA[:, 4:8:2, :], ALU.mult))

                for j, st in enumerate(({4: [dt_abs], 5: [dt_u], 6: [dt_end]},
                                        {4: [lambda: conv_bc(1)], 5: [cumulative], 8: [decay_dt]})):
                    st[12] = [lambda: conv_bc(2 * j)]
                    halves(base + PH_BC + j * 2, st)
                    halves(base + PH_BC + j * 2 + 1, st, first=8)
                ch.reset()

                def ssd_steps(q):
                    G = L * NG + q

                    def masks():
                        dve.wait_ge(s_("cb_done"), G + 1)
                        dve.wait_ge(s_("y_part"), G * HG + ONE)
                        dve.tensor_copy(CB[:].rearrange("p s n -> p (s n)"), A[:, 2, 0:256]).then_inc(s_("cb_ready"), 1)
                        dve.wait_ge(s_("H_hi"), G + 1)
                        Hl = H[64:128].rearrange("p d s n -> p (d s n)")
                        tt(Hl, A[64:128, 3, :], Hl.bitcast(F32), ALU.subtract).then_inc(s_("H_ready"), 1)

                    def M(h):
                        dve.wait_ge(s_("exp_done"), G * HG + h + 1)
                        if h == 0:
                            dve.wait_ge(s_("cb_ready"), G + 1)
                        for d in range(2):
                            for s in range(2):
                                e = E[h % 2][:, d, s, :]
                                ins = dve.scalar_tensor_tensor(out=e, in0=e, scalar=gs[:, 4 + 2 * d + s, h:h + 1],
                                                               in1=CB[:, s, :], op0=ALU.mult, op1=ALU.mult)
                        ins.then_inc(s_("M_ready"), 1)

                    def add_y():
                        dve.wait_ge(s_("yD_ready"), G + 1)
                        dve.wait_ge(s_("y_part"), G * HG + HG + ONE)
                        ch.link(tt(y[:], y[:], A[:, 0:2, :], ALU.add))
                        dve.wait_ge(s_("yoff_done"), G + 1)
                        for d in range(2):
                            ch.wait()
                            ins = tt(yoff.rearrange("p (h n) -> p h n", h=HG), A[:, 2 + d, :].rearrange("p (h n) -> p h n", h=HG),
                                     gs[:, 14 + d, :].unsqueeze(2).to_broadcast([P, HG, HP]), ALU.mult)
                            if d == 0:
                                ch.link(ins)
                                ch.wait()
                            else:
                                ins.then_inc(s_("yoff_read"), 1)
                                dve.wait_ge(s_("yoff_read"), G + 1)
                            ch.link(tt(y[:, 1], y[:, 1], yoff, ALU.add))
                        ch.wait()
                        tt(y[:], y[:], zs[:], ALU.mult).then_inc(s_("yz_ready"), 1)

                    def scale_y():
                        dve.wait_ge(s_("yrstd_ready"), G + 1)
                        for s in range(2):
                            ins = dve.tensor_scalar(y[:, s], y[:, s], rstd[:, s:s + 1], None, ALU.mult)
                        ins.then_inc(s_("yn_ready"), 1)

                    def y_lo():
                        dve.wait_ge(s_("y_hi"), G + 1)
                        for t in range(4):
                            sl = span(q * 4 + t, 1)
                            ins = dve.scalar_tensor_tensor(out=yT_l[:, sl, :],
                                                           in0=A[:, t // 2:t // 2 + 1, (t % 2) * 256:(t % 2 + 1) * 256],
                                                           scalar=nrm[0][:, t:t + 1], in1=yT_h[:, sl, :].bitcast(F32),
                                                           op0=ALU.mult, op1=ALU.subtract)
                        ins.then_inc(s_("yT_read"), 1)
                    st = {3: [masks], 14: [add_y], 15: [scale_y, y_lo]}
                    for h in range(HG):
                        st.setdefault(4 + h, []).append(lambda h=h: M(h))
                    return st

                def conv_1(g):
                    dve.wait_ge(s_("conv_center"), L * 12 + 4 + g + 1)
                    conv_taps(0, 0, (0, 1))

                def conv_2(g):
                    conv_taps(0, 0, (3, 4))
                    dve.wait_ge(bank_free[0], ub + U_SSD + g + 2)
                    dve.sem_inc(s_("conv_done"), 1)

                def ssd_body(g, steps):
                    st = {k: list(v) for k, v in steps.items()}
                    st[12] = [lambda: conv_1(g)] + st.get(12, [])
                    st[13] = [lambda: conv_2(g)] + st.get(13, [])
                    halves(base + PH_SSD + g * 2, st)
                    halves(base + PH_SSD + g * 2 + 1, st, first=8)
                    ch.reset()
                ssd_body(0, {4: [lambda: conv_bc(3)], 5: [lambda: end_phase(dve)]})
                with dve.Fori(1, NG) as g:
                    ssd_body(g, ssd_steps(g - 1))
                end_phase(dve)

                def gate_s(q):
                    chunk_done(dve, base + PH_PS + q * 3 + 1, 16)
                    dve.wait_ge(s_("sg_ready"), L * 8 + q + 1)
                    dve.wait_ge(s_("yT_read"), L * NG + NG + ONE)
                    cs = span(q * N, N)
                    ins = tt(x2[:, :, cs], PM[:, 2:4, :], sg[:], ALU.mult)
                    ins.then_inc(s_("sg_used"), 1)
                    dve.wait_ge(s_("sg_used"), L * 8 + q + 1 + ONE)
                    dve.sem_inc(bank_free[1], 1)
                def ps_body(j, steps):
                    halves(base + PH_PS + j * 3, steps)
                    halves(base + PH_PS + j * 3 + 1, steps, first=8, n_halves=16)
                ps_body(0, ssd_steps(NG - 1))
                ch.reset()
                with dve.Fori(1, 4) as j:
                    ps_body(j, {4: [lambda: gate_s(j - 1)]})

                def last_gate():
                    gate_s(3)
                    end_phase(dve)

                def k_rope():
                    after_phase(dve, L, 5)
                    chunk_done(dve, base + PH_KV)
                    dve.wait_ge(s_("kc_ready"), L + 1)
                    rope(PM[:, 1], qt[:, 1]).then_inc(s_("k_ready"), 1)
                    dve.wait_ge(s_("k_ready"), L + 1)
                    dve.sem_inc(bank_free[0], 1)
                halves(base + PH_KV, {4: [last_gate]})
                halves(base + PH_KV + 1, {4: [k_rope]})
                ch.reset()
                end_phase(dve)

                def q_rope(g):
                    G = L * 4 + g
                    chunk_done(dve, base + PH_Q + g * 2)
                    dve.wait_ge(s_("qc_ready"), G + 1)
                    dve.wait_ge(s_("q_T"), G + ONE)
                    dve.wait_ge(s_("o_done"), G + ONE)
                    rope(PM[:, 1], qt[:, 1]).then_inc(s_("q_ready"), 1)
                    dve.wait_ge(s_("q_ready"), G + 1)
                    dve.sem_inc(bank_free[0], 1)

                def maxima(g):
                    G = L * 4 + g
                    dve.wait_ge(s_("scores_done"), G + 1 + ONE)
                    dve.tensor_reduce(sm[:, 0, 0:4], A[:, 2, :].rearrange("p (h n) -> p h n", h=4), AX_X, ALU.max)
                    ch.link(dve.tensor_reduce(sm[:, 0, 4:8], A[:, 0:2, :].rearrange("p b (h n) -> p (b h) n", h=2), AX_X, ALU.max))
                    ch.wait()
                    sk = sink[:, span(g * 4, 4)]
                    sk = sk.unsqueeze(1).to_broadcast([P, 2, 4])
                    v = lambda r: sm[:, r].rearrange("p (s h) -> p s h", s=2)
                    ch.link(dve.scalar_tensor_tensor(out=v(1), in0=v(0), scalar=SCALE, in1=sk, op0=ALU.mult, op1=ALU.max))
                    ch.wait()
                    ch.link(dve.tensor_scalar(sm[:, 1], sm[:, 1], -1.0, None, ALU.mult))
                    ch.wait()
                    tt(v(3), v(1), sk, ALU.add).then_inc(s_("nm_ready"), 1)

                def normalize(g):
                    G = L * 4 + g
                    dve.wait_ge(s_("exps_done"), G + 1)
                    ch.link(tt(sm[:, 5], sm[:, 2], sm[:, 4], ALU.add))
                    ch.wait()
                    ch.link(dve.reciprocal(sm[:, 5], sm[:, 5]))
                    ch.wait()
                    tt(Pc[:], Pc[:], sm[:, 5, 0:4].unsqueeze(2).to_broadcast([P, 4, P]), ALU.mult)
                    tt(Pl[:], Pl[:], sm[:, 5, 4:8].unsqueeze(2).to_broadcast([P, 4, 256]), ALU.mult).then_inc(s_("p_ready"), 1)

                def attn_steps(q):
                    G = L * 4 + q

                    def a_mul():
                        dve.wait_ge(s_("o_done"), G + 1 + ONE)
                        dve.wait_ge(bank_free[1], ub + U_Q + q + 2)
                        zv = zaT.rearrange("p (h s n) -> p h s n", h=4, s=2)
                        for s in range(2):
                            ins = tt(zv[:, :, s], A[:, 3 - s, :].rearrange("p (h n) -> p h n", h=4), zv[:, :, s], ALU.mult)
                        ins.then_inc(s_("a_read"), 1)
                        dve.wait_ge(s_("a_hi"), G + 1)
                        sl = span(q * 4, 4)
                        tt(aT_l[:, sl, :], zaT.rearrange("p (k n) -> p k n", k=4), aT_h[:, sl, :].bitcast(F32), ALU.subtract)\
                            .then_inc(s_("aT_ready"), 1)
                    return {4: [lambda: maxima(q)], 5: [lambda: normalize(q)], 8: [a_mul]}

                def q_body(g, steps):
                    st = {k: list(v) for k, v in steps.items()}
                    st[12] = [lambda: q_rope(g)]
                    halves(base + PH_Q + g * 2, st)
                    halves(base + PH_Q + g * 2 + 1, st, first=8)
                    ch.reset()
                q_body(0, {11: [lambda: after_phase(dve, L, 6)]})
                with dve.Fori(1, 4) as g:
                    q_body(g, attn_steps(g - 1))
                end_phase(dve)

                def merge(q):
                    G = L * 4 + q
                    chunk_done(dve, base + PH_PA + q * (3 if more else 2) + 1, 15 if more else 8)
                    dve.wait_ge(s_("sg_ready"), L * 8 + q + 4 + 1)
                    dve.wait_ge(s_("m_T"), G + ONE)
                    tt(m32[:], PM[:, 2:4, :], sg[:], ALU.mult).then_inc(s_("sg_used"), 1)
                    dve.wait_ge(s_("sg_used"), L * 8 + q + 4 + 1 + ONE)
                    dve.sem_inc(bank_free[1], 1)
                    cs = span(q * N, N)
                    tt(m32[:], m32[:], x2[:, :, cs], ALU.add).then_inc(s_("m_ready"), 1)

                def m_lo(q):
                    dve.wait_ge(s_("m_hi"), L * 4 + q + 1)
                    sl = span(q * 4, 4)
                    tt(mT_l[:, sl, :], m_banks(q).rearrange("p b (k n) -> p (b k) n", k=2), mT_h[:, sl, :].bitcast(F32),
                       ALU.subtract).then_inc(s_("mT_ready"), 1)

                kn = kb + MOD_GATE

                def pa_body(j, steps):
                    c = base + PH_PA + j * (3 if more else 2)
                    halves(c, steps)
                    halves(c + 1, steps, first=8, mod=more)
                pa_body(0, attn_steps(3))
                ch.reset()
                with dve.Fori(1, 4) as j:
                    st = {3: [lambda: merge(j - 1)], 7: [lambda: m_lo(j - 1)]}
                    if more:
                        st[6] = [lambda: mod_fin(dve, A, 1, kn + j - 1)]
                    pa_body(j, st)

                def resid(j, par):
                    if j == 0 and par == 0:
                        after_phase(dve, L, 8)
                    w_out_chunk = base + ph_out(more) + (j * 2 + par) * (2 if more else 1)
                    dve.wait_ge(w_used, 8 * w_out_chunk + (15 if more else 8) + CR)
                    dve.wait_ge(s_(f"gb_loaded{par}"), (L * 2 + j + 1) * 4 * DMA)
                    tt(gb[par][:], PM[:, 2 * par:2 * par + 2, :], gb[par][:], ALU.mult).then_inc(bank_free[par], 1)
                    dve.wait_ge(bank_free[par], ub + U_OUT + j + 2)
                    tt(x2[:, :, span(j * (2 * N) + par * N, N)], gb[par][:], xch[par][:], ALU.add).then_inc(s_("xnew"), 1)

                for j in range(2):
                    c = base + ph_out(more) + j * (4 if more else 2)
                    for par in range(2):
                        kk = kn + 4 + j * 2 + par
                        st = {5: [lambda: mod_fin(dve, A, 1 - par, kk - 1)]} if more else {}
                        if j == 0 and par == 0:
                            st[3] = [lambda: merge(3)]
                            st[6] = [lambda: m_lo(3), lambda: end_phase(dve)]
                        else:
                            st[4] = [lambda: resid(*((j, 0) if par else (0, 1)))]
                        halves(c + par * (2 if more else 1), st, mod=more)
                resid(1, 1)
                if more:
                    mod_fin(dve, A, 1, kn + 7)
                end_phase(dve)

            with dve.Fori(0, DEPTH - 1) as layer_index:
                layer(layer_index, True)
            layer(DEPTH - 1, False)

            after_phase(dve, DEPTH, 0)
            dve.wait_ge(s_("rstd_ready"), DEPTH + 1)
            dve.wait_ge(s_("fng_loaded"), DMA)
            for s in range(2):
                ins = dve.scalar_tensor_tensor(out=x2[:, s], in0=x2[:, s], scalar=rstd[:, s:s + 1], in1=fng,
                                               op0=ALU.mult, op1=ALU.mult)
            ins.then_inc(s_("y_final"), 1)

        @block.gpsimd
        def _(pool):
            me[0] = "pool"
            start_at_one(pool)
            ch = Chain(pool, pool_chain)
            ch.link(pool.memset(dAg[:], 0.0))
            ch.wait()
            ch.reset()
            pool.dma_start(cst[:], a["cst"]).then_inc(s_("const_loaded"), DMA)
            for s, v in enumerate((a["c_ctx"], a["c"][0])):
                pool.dma_start(cvec[:, s], v.rearrange("(p k) -> p k", k=KT)).then_inc(s_("cvec_loaded"), DMA)
            for s, v in enumerate((a["x_prompt"][0], a["x_sample"][0])):
                pool.dma_start(x2[:, s], v).then_inc(s_("x_loaded"), DMA)
                pool.dma_start(x_dram[s], v).then_inc(s_("x_copied"), DMA)
            wait_alone(pool, s_("x_loaded"), 2 * DMA)
            wait_alone(pool, s_("x_copied"), 2 * DMA)
            wait_alone(pool, s_("half_exp_set"), 1)
            end_phase(pool)

            def rms(count, width, ready, done):
                wait_alone(pool, s_(ready), count)
                ch.link(pool.tensor_scalar(rstd[:], sm[:, 0, 0:2], 1.0 / width, EPS, ALU.mult, ALU.add))
                ch.wait()
                pool.tensor_tensor(rstd[:], rstd[:], half_exp[:], ALU.pow).then_inc(s_(done), 1)

            with pool.Fori(0, MOD_FIRST) as j:
                mod_io(pool, j + 0, 0, j * N)

            def layer(L, more):
                kn = mod_first(L) + MOD_GATE
                after_phase(pool, L, 0)
                pool.sem_inc(s_("x_ready"), 1)
                cv = a["conv_w"][L].rearrange("j (t c) -> (j t) c", c=P)
                pool.dma_start(rows[0:120, 0], cv[0:120, :]).then_inc(s_("rows_loaded"), DMA)
                pool.dma_start(rows[0:120, 1], cv[120:240, :]).then_inc(s_("rows_loaded"), DMA)
                pool.dma_start(rows[0:48, 2], a["conv_b"][L].rearrange("(t c) -> t c", c=P)).then_inc(s_("rows_loaded"), DMA)
                pool.dma_start(rows[48:80, 2], a["ssd_norm_g"][L].rearrange("(t c) -> t c", c=P)).then_inc(s_("rows_loaded"), DMA)

                def bcast(v, n):
                    return v.unsqueeze(0).to_broadcast([P, n])
                for d, (al, db) in enumerate((("a_log_fwd", "dt_bias_fwd"), ("a_log_bwd", "dt_bias_bwd"))):
                    pool.dma_start(arow[:, d * NH:(d + 1) * NH], bcast(a[al][L], NH)).then_inc(s_("small_loaded"), DMA)
                    pool.dma_start(dtb[:, d * NH:(d + 1) * NH], bcast(a[db][L], NH)).then_inc(s_("small_loaded"), DMA)
                pool.dma_start(SA[:, 16, :], bcast(a["d_skip"][L], NH)).then_inc(s_("small_loaded"), DMA)
                pool.dma_start(ng[:], a["norm_g"][L].rearrange("(p k) -> p k", k=KT)).then_inc(s_("small_loaded"), DMA)
                pool.dma_start(sink[:], bcast(a["attn_sink"][L], N_Q)).then_inc(s_("sink_loaded"), DMA)
                for s in range(2):
                    for w in range(2):
                        pool.dma_start(mcol[:, s, w], mod_dram[s, w * D_MODEL:(w + 1) * D_MODEL].rearrange("(p k) -> p k", k=KT))\
                            .then_inc(s_("mcol_loaded"), DMA)
                rms(L + 1, D_MODEL, "ss_ready", "rstd_ready")
                with pool.Fori(0, MOD_GATE) as j:
                    mod_io(pool, mod_first(L) + j, L, j * N + 2 * D_MODEL)
                ch.reset()
                end_phase(pool)
                end_phase(pool)

                def copy_cw(k, tile, buf):
                    return pool.tensor_copy(cw[buf][:], chw[:, 0:288].rearrange("p (j t) -> p j t", j=6)[:, :, span(tile, 4)])
                wait_alone(pool, s_("chw_ready"), L + 1)
                with pool.Fori(0, 2) as j:
                    for par in range(2):
                        k = L * 12 + j * 2 + par
                        wait_alone(pool, s_("conv_done"), k + ONE)
                        copy_cw(k, j * 8 + 32 + par * 4, par).then_inc(s_("cw_copied"), 1)
                end_phase(pool)
                after_phase(pool, L, 3)

                def ssd_group(q, more):
                    G = L * NG + q
                    for w in range(2):
                        pool.tensor_copy(BCg[:, w:w + 1, :], BC[:, span(q + 8 * w, 1), :])
                    for w in range(2):
                        pool.tensor_copy(dAg[:, :, 64 * w:64 * w + HG], SA[:, 8:12, span(q * HG, HG)])
                    pool.tensor_copy(gs[:], SA[:, :, span(q * HG, HG)]).then_inc(s_("group_copied"), 1)
                    tiles = span(q * 4 + 288, 4)
                    pool.tensor_copy(nrm[0][:], chw[:, tiles]).then_inc(s_("nrm_copied"), 1)
                    for d, st in enumerate(("state_ssm_fwd", "state_ssm_bwd")):
                        src = a[st][0, L, span(q * HG, HG)].rearrange("h r n -> (h r) n").rearrange("(t p) n -> p t n", p=P)
                        pool.dma_start(stload[:, d], src).then_inc(s_("st_loaded"), DMA)
                    if more:
                        next_cw(q + 1)
                    wait_alone(pool, s_("group_copied"), G + 1)
                    wait_alone(pool, s_("xt_ready"), G + 1 + ONE)
                    hv = "p (h n) -> p h n"
                    for s in range(2):
                        ins = pool.tensor_tensor(y[:, s].rearrange(hv, h=HG), xt[:, s].rearrange(hv, h=HG),
                                                 gs[:, 16, :].unsqueeze(2).to_broadcast([P, HG, HP]), ALU.mult)
                    ins.then_inc(s_("yD_ready"), 1)
                    for d in range(2):
                        ins = pool.tensor_tensor(xw[:, d].rearrange(hv, h=HG), xt[:, 0].rearrange(hv, h=HG),
                                                 gs[:, 12 + d, :].unsqueeze(2).to_broadcast([P, HG, HP]), ALU.mult)
                    ins.then_inc(s_("xw_ready"), 1)
                    wait_alone(pool, s_("st_stored"), G + 1 + ONE)
                    for d, st in enumerate(("state_f_out", "state_b_out")):
                        dst = o[st][0, L, span(q * HG, HG)].rearrange("h r n -> (h r) n").rearrange("(t p) n -> p t n", p=P)
                        pool.dma_start(dst, ST[:, d].rearrange("p (t n) -> p t n", t=4)).then_inc(s_(("st_out", "st_out_b")[d]), DMA)
                    rms(G + 1, SSD_WIDTH // NG, "yss_ready", "yrstd_ready")
                    wait_alone(pool, s_("st_out"), (G + 1) * DMA)
                    wait_alone(pool, s_("st_out_b"), (G + 1) * DMA)
                    pool.sem_inc(s_("ST_free"), 1)
                    wait_alone(pool, s_("yT_read"), G + 1 + ONE)
                    ch.reset()

                def next_cw(g):
                    wait_alone(pool, s_("conv_done"), L * 12 + 4 + g + ONE)
                    copy_cw(g, g * 4, 0).then_inc(s_("cw_copied"), 1)
                next_cw(0)
                with pool.Fori(0, NG - 1) as g:
                    ssd_group(g, True)
                ssd_group(NG - 1, False)
                end_phase(pool)
                end_phase(pool)
                after_phase(pool, L, 5)
                kc = a["cache_k"][0, L].rearrange("t h d -> t (h d)")
                vc = a["cache_v"][0, L].rearrange("t h d -> t (h d)")
                pool.dma_start(kraw, kc).then_inc(s_("kv_loaded"), DMA)
                pool.dma_start(vA[:, 0], vc).then_inc(s_("kv_loaded"), DMA)
                wait_alone(pool, s_("kc_ready"), L + 1)
                pool.dma_start(o["k_out"][0, L].rearrange("t h d -> t (h d)"), qt[:, 0]).then_inc(s_("k_out"), DMA)
                wait_alone(pool, s_("k_out"), (L + 1) * DMA)
                end_phase(pool)
                after_phase(pool, L, 6)
                pool.dma_start(o["v_out"][0, L].rearrange("t h d -> t (h d)"), vA[:, 2]).then_inc(s_("v_out"), DMA)
                with pool.Fori(0, 4) as g:
                    wait_alone(pool, s_("o_done"), L * 4 + g + ONE)
                    pool.tensor_copy(vg[:], vA[:, :, span(g * P, P)]).then_inc(s_("vg_ready"), 1)
                wait_alone(pool, s_("v_out"), (L + 1) * DMA)
                wait_alone(pool, s_("sink_loaded"), (L + 1) * DMA)
                end_phase(pool)
                wait_alone(pool, s_("aT_ready"), L * 4 + 4 + ONE)
                if more:
                    with pool.Fori(0, 4) as j:
                        mod_io(pool, kn + j, L + 1, j * N)
                end_phase(pool)
                after_phase(pool, L, 8)

                def gate_and_x(j, par):
                    for s in range(2):
                        gate = mod_dram[s, span(j * (2 * N) + 2 * D_MODEL + par * N, N)]
                        pool.dma_start(gb[par][:, s], gate.unsqueeze(0).to_broadcast([P, N])).then_inc(s_(f"gb_loaded{par}"), DMA)
                        pool.dma_start(xch[par][:, s], x_dram[s, :, span(j * (2 * N) + par * N, N)]).then_inc(s_(f"gb_loaded{par}"), DMA)

                with pool.Fori(0, 2) as j:
                    wait_alone(pool, s_("xnew"), (L * 4 + j * 2) + ONE)
                    for par in range(2):
                        gate_and_x(j, par)
                    for par in range(2):
                        if more:
                            mod_io(pool, kn + 4 + j * 2 + par, L + 1, j * (2 * N) + (4 + par) * N)
                    for par in range(2):
                        cs = span(j * (2 * N) + par * N, N)
                        wait_alone(pool, s_("xnew"), L * 4 + j * 2 + par + 1 + ONE)
                        for s in range(2):
                            pool.dma_start(x_dram[s, :, cs], x2[:, s, cs]).then_inc(s_("x_stored"), DMA)
                    wait_alone(pool, s_("x_stored"), (L * 8 + j * 4 + 4) * DMA)
                end_phase(pool)

            with pool.Fori(0, DEPTH - 1) as layer_index:
                layer(layer_index, True)
            layer(DEPTH - 1, False)

            after_phase(pool, DEPTH, 0)
            pool.dma_start(fng, a["final_norm_g"].unsqueeze(0).to_broadcast([P, D_MODEL])).then_inc(s_("fng_loaded"), DMA)
            rms(DEPTH + 1, D_MODEL, "ss_ready", "rstd_ready")
            wait_alone(pool, s_("y_final"), 1)
            for s, v in enumerate((o["y_prompt"][0], o["y_sample"][0])):
                pool.dma_start(v, x2[:, s]).then_inc(s_("y_out"), DMA)
            wait_alone(pool, s_("y_out"), 2 * DMA)


_INS = ["x_prompt", "x_sample", "c", "cache_k", "cache_v", "state_ssm_fwd", "state_ssm_bwd", "c_ctx", "norm_g", "w_mod",
        "b_mod", "w_in", "conv_w", "conv_b", "attn_sink", "a_log_fwd", "a_log_bwd", "dt_bias_fwd", "dt_bias_bwd", "d_skip",
        "ssd_norm_g", "w_pa", "w_ps", "w_out", "final_norm_g"]
_OUTS = [("y_prompt", (1, TOK, D_MODEL)), ("y_sample", (1, TOK, D_MODEL)),
         ("k_out", (1, DEPTH, TOK, N_KV, HEAD_DIM)), ("v_out", (1, DEPTH, TOK, N_KV, HEAD_DIM)),
         ("state_f_out", (1, DEPTH, NH, HP, D_STATE)), ("state_b_out", (1, DEPTH, NH, HP, D_STATE))]


def kernel(**inputs):
    import numpy as np
    import concourse.bacc as bacc
    from concourse.bass_utils import run_bass_kernel_spmd

    nc = bacc.Bacc("TRN2", target_bir_lowering=False, num_devices=1, dynamic_dma_scratch_size=8192)
    arrays, a = {}, {}
    inputs = dict(inputs, cst=constants())
    for name in _INS + ["cst"]:
        v = np.ascontiguousarray(inputs[name])
        arrays[f"in_{name}"] = v
        a[name] = nc.dram_tensor(f"in_{name}", v.shape, F32, kind="ExternalInput").ap()
    o = {n: nc.dram_tensor(f"out_{n}", s, F32, kind="ExternalOutput").ap() for n, s in _OUTS}
    build(nc, a, o)
    r = run_bass_kernel_spmd(nc, [arrays], core_ids=[0])
    return tuple(r.results[0][f"out_{n}"] for n, _ in _OUTS)
```
